# Optimizing a Trainium2 kernel written in Bass

```python
import math
import jax, jax.numpy as jnp
from jax import lax
import numpy as np

D_MODEL = 1024
BATCH = 1
SEQ = 512
DEPTH = 1

MIX_WIDTH = D_MODEL
SB_WIDTH = D_MODEL // 2
SB_HEADS = 8
SB_HEAD_DIM = SB_WIDTH // SB_HEADS
POOL_WIDTH = MIX_WIDTH - SB_WIDTH
POOL_WINDOWS = (2, 4, 8, 16)
POOL_GROUPS = len(POOL_WINDOWS)
POOL_GROUP_DIM = POOL_WIDTH // POOL_GROUPS
IN_WIDTH = 3 * SB_WIDTH + POOL_WIDTH
D_FF = -(-8 * D_MODEL // (3 * 256)) * 256
Q_BLOCK = 128
N_MOD = 6
EPS = 1e-6


def rmsnorm(x, g):
    xf = x.astype(jnp.float32)
    y = xf * lax.rsqrt(jnp.mean(xf * xf, axis=-1, keepdims=True) + EPS)
    return (y * g.astype(jnp.float32)).astype(x.dtype)

def stick_breaking_attention(q, k, v):
    S = q.shape[2]
    inv_sqrt = 1.0 / math.sqrt(q.shape[-1])
    outs = []
    for i in range(S // Q_BLOCK):
        L = (i + 1) * Q_BLOCK
        qb = q[:, :, i * Q_BLOCK:L].astype(jnp.float32)
        kb = k[:, :, :L].astype(jnp.float32)
        vb = v[:, :, :L].astype(jnp.float32)
        z = jnp.einsum('bhqd,bhkd->bhqk', qb, kb) * inv_sqrt
        t_idx = i * Q_BLOCK + jnp.arange(Q_BLOCK)[:, None]
        s_idx = jnp.arange(L)[None, :]
        mask = s_idx < t_idx
        log1m = jnp.where(mask, -jax.nn.softplus(z), 0.0)
        after = lax.cumsum(log1m, axis=3, reverse=True) - log1m
        logw = jax.nn.log_sigmoid(z) + after
        w = jnp.where(mask, jnp.exp(jnp.where(mask, logw, 0.0)), 0.0)
        outs.append(jnp.einsum('bhqk,bhkd->bhqd', w, vb))
    return jnp.concatenate(outs, axis=2).astype(v.dtype)

def pooling_mixer(u, w_pool, pool_scale):
    B, S, P = u.shape
    uf = u.astype(jnp.float32)
    cs = jnp.concatenate([jnp.zeros((B, 1, P), jnp.float32), jnp.cumsum(uf, axis=1)], axis=1)
    t = jnp.arange(S)
    parts = []
    for g, win in enumerate(POOL_WINDOWS):
        sl = slice(g * POOL_GROUP_DIM, (g + 1) * POOL_GROUP_DIM)
        lo = jnp.maximum(t + 1 - win, 0)
        cnt = (t + 1 - lo).astype(jnp.float32)
        csg = cs[..., sl]
        mean = (csg[:, 1:] - csg[:, lo]) / cnt[None, :, None]
        parts.append(mean - uf[..., sl])
    pooled = jnp.stack(parts, axis=2)
    y = jnp.einsum('bsgc,gcd->bsgd', pooled, w_pool.astype(jnp.float32)).reshape(B, S, P)
    return (y * pool_scale.astype(jnp.float32)).astype(u.dtype)

def first_inputs(seed: int = 0) -> dict:
    key = jax.random.key(seed)
    ks = jax.random.split(key, 16)
    f32 = jnp.float32

    def nrm(k, shape, fan_in):
        return jax.random.normal(k, shape, f32) * fan_in ** -0.5

    def gain(k):
        return 1.0 + 0.05 * jax.random.normal(k, (DEPTH, D_MODEL), f32)

    return {
        "x": jax.random.normal(ks[0], (BATCH, SEQ, D_MODEL), f32),
        "c": jax.random.normal(ks[1], (BATCH, D_MODEL), f32),
        "w_cond": nrm(ks[2], (DEPTH, D_MODEL, N_MOD * D_MODEL), D_MODEL),
        "b_cond": 0.01 * jax.random.normal(ks[3], (DEPTH, N_MOD * D_MODEL), f32),
        "g_mix_pre": gain(ks[4]),
        "g_mix_post": gain(ks[5]),
        "w_in": nrm(ks[6], (DEPTH, D_MODEL, IN_WIDTH), D_MODEL),
        "w_pool": nrm(ks[7], (DEPTH, POOL_GROUPS, POOL_GROUP_DIM, POOL_GROUP_DIM), POOL_GROUP_DIM),
        "pool_scale": 1.0 + 0.1 * jax.random.normal(ks[8], (DEPTH, POOL_WIDTH), f32),
        "w_out": nrm(ks[9], (DEPTH, MIX_WIDTH, D_MODEL), MIX_WIDTH),
        "g_ffn_pre": gain(ks[10]),
        "g_ffn_post": gain(ks[11]),
        "w_gate": nrm(ks[12], (DEPTH, D_MODEL, D_FF), D_MODEL),
        "w_up": nrm(ks[13], (DEPTH, D_MODEL, D_FF), D_MODEL),
        "w_down": nrm(ks[14], (DEPTH, D_FF, D_MODEL), D_FF),
    }

def first_block(x, c, w_cond, b_cond, g_mix_pre, g_mix_post, w_in, w_pool, pool_scale,
              w_out, g_ffn_pre, g_ffn_post, w_gate, w_up, w_down):
    B, S, D = x.shape
    for l in range(DEPTH):
        mod = jax.nn.silu(c) @ w_cond[l] + b_cond[l]
        shift_m, scale_m, gate_m, shift_f, scale_f, gate_f = [
            m[:, None, :] for m in jnp.split(mod, N_MOD, axis=-1)]

        h = rmsnorm(x, g_mix_pre[l]) * (1.0 + scale_m) + shift_m
        proj = h @ w_in[l]
        q, k, v, u = jnp.split(proj, [SB_WIDTH, 2 * SB_WIDTH, 3 * SB_WIDTH], axis=-1)
        to_heads = lambda a: a.reshape(B, S, SB_HEADS, SB_HEAD_DIM).transpose(0, 2, 1, 3)
        attn = stick_breaking_attention(to_heads(q), to_heads(k), to_heads(v))
        attn = attn.transpose(0, 2, 1, 3).reshape(B, S, SB_WIDTH)
        pool = pooling_mixer(u, w_pool[l], pool_scale[l])
        mix = jnp.concatenate([attn, pool], axis=-1) @ w_out[l]
        x = x + gate_m * rmsnorm(mix, g_mix_post[l])

        h = rmsnorm(x, g_ffn_pre[l]) * (1.0 + scale_f) + shift_f
        f = (jax.nn.silu(h @ w_gate[l]) * (h @ w_up[l])) @ w_down[l]
        x = x + gate_f * rmsnorm(f, g_ffn_post[l])
    return x


CHUNK = 64
SSD_EXPAND = 2
SSD_INNER = SSD_EXPAND * D_MODEL
SSD_HEAD_DIM = 64
SSD_HEADS = SSD_INNER // SSD_HEAD_DIM
SSD_GROUPS = 4
SSD_HPG = SSD_HEADS // SSD_GROUPS
SSD_STATE = 128
SSD_CONV = 4
SSD_XBC = SSD_INNER + 2 * SSD_GROUPS * SSD_STATE
SCONV_DIM = D_MODEL
SCONV_K = 3
FFN_HIDDEN = ((8 * D_MODEL + 767) // 768) * 256
IN_SIZES = (SSD_INNER, SSD_XBC, SSD_HEADS, SCONV_DIM, SCONV_DIM, SCONV_DIM, D_MODEL, D_MODEL)
IN_DIM = sum(IN_SIZES)
IN_SPLITS = tuple(int(v) for v in np.cumsum(IN_SIZES)[:-1])


def rmsnorm_2(x, w):
    x32 = x.astype(jnp.float32)
    y = x32 * lax.rsqrt(jnp.mean(x32 * x32, axis=-1, keepdims=True) + EPS)
    return (y * w.astype(jnp.float32)).astype(x.dtype)

def causal_depthwise_conv(x, w):
    k = w.shape[0]
    return lax.conv_general_dilated(
        x, w[:, None, :].astype(x.dtype), window_strides=(1,), padding=[(k - 1, 0)],
        dimension_numbers=('NWC', 'WIO', 'NWC'), feature_group_count=x.shape[-1])

def ssd_chunked_scan(x, dt, a, bm, cm):
    bsz, seqlen = x.shape[0], x.shape[1]
    nc = seqlen // CHUNK

    def to_chunks(t):
        return jnp.moveaxis(t.reshape((bsz, nc, CHUNK) + t.shape[2:]), 1, 0)

    causal = jnp.tril(jnp.ones((CHUNK, CHUNK), dtype=bool))[None, :, :, None, None]

    def step(state, inp):
        xc, dtc, bc, cc = inp
        acum = jnp.cumsum(dtc * a, axis=1)
        seg = acum[:, :, None] - acum[:, None, :]
        decay = jnp.exp(jnp.where(causal, seg, -jnp.inf))
        cb = jnp.einsum('blgn,bsgn->blsg', cc, bc)
        xdt = xc * dtc[..., None]
        scores = cb[..., None] * decay
        y_diag = jnp.einsum('blsgr,bsgrp->blgrp', scores, xdt)
        y_off = jnp.einsum('blgn,bgrpn->blgrp', cc, state) * jnp.exp(acum)[..., None]
        to_end = jnp.exp(acum[:, -1:] - acum)
        new_state = (state * jnp.exp(acum[:, -1])[..., None, None]
                     + jnp.einsum('bsgn,bsgr,bsgrp->bgrpn', bc, to_end, xdt))
        return new_state, y_diag + y_off

    state0 = jnp.zeros((bsz, SSD_GROUPS, SSD_HPG, SSD_HEAD_DIM, SSD_STATE), jnp.float32)
    _, ys = lax.scan(step, state0, (to_chunks(x), to_chunks(dt), to_chunks(bm), to_chunks(cm)))
    return jnp.moveaxis(ys, 0, 1).reshape(x.shape)

def hybrid_mixer(h, w_in, ssd_conv_w, ssd_conv_b, dt_bias, a_log, d_skip, ssd_norm_w,
                 w_ssd_proj, sconv_w, w_sconv_proj, w_o):
    bsz, seqlen, _ = h.shape
    u = h @ w_in
    z, xbc, dt_raw, s_b, s_c, s_x, g_a, g_b = jnp.split(u, IN_SPLITS, axis=-1)

    xbc = jax.nn.silu(causal_depthwise_conv(xbc, ssd_conv_w) + ssd_conv_b)
    xs, bm, cm = jnp.split(xbc, (SSD_INNER, SSD_INNER + SSD_GROUPS * SSD_STATE), axis=-1)
    xs32 = xs.astype(jnp.float32).reshape(bsz, seqlen, SSD_GROUPS, SSD_HPG, SSD_HEAD_DIM)
    dt = jax.nn.softplus(dt_raw.astype(jnp.float32) + dt_bias.astype(jnp.float32))
    dt = dt.reshape(bsz, seqlen, SSD_GROUPS, SSD_HPG)
    a = -jnp.exp(a_log.astype(jnp.float32)).reshape(SSD_GROUPS, SSD_HPG)
    bm32 = bm.astype(jnp.float32).reshape(bsz, seqlen, SSD_GROUPS, SSD_STATE)
    cm32 = cm.astype(jnp.float32).reshape(bsz, seqlen, SSD_GROUPS, SSD_STATE)
    y = ssd_chunked_scan(xs32, dt, a, bm32, cm32)
    y = y + d_skip.astype(jnp.float32).reshape(SSD_GROUPS, SSD_HPG)[..., None] * xs32
    y = y.reshape(bsz, seqlen, SSD_INNER) * jax.nn.silu(z.astype(jnp.float32))
    yg = y.reshape(bsz, seqlen, SSD_GROUPS, SSD_INNER // SSD_GROUPS)
    yg = yg * lax.rsqrt(jnp.mean(yg * yg, axis=-1, keepdims=True) + EPS)
    y = (yg.reshape(bsz, seqlen, SSD_INNER) * ssd_norm_w.astype(jnp.float32)).astype(h.dtype)
    branch_a = y @ w_ssd_proj

    v = causal_depthwise_conv(s_c * s_x, sconv_w)
    branch_b = (s_b * v) @ w_sconv_proj

    merged = jax.nn.sigmoid(g_a) * branch_a + jax.nn.sigmoid(g_b) * branch_b
    return merged @ w_o

def swiglu(h, w_gate, w_up, w_down):
    return (jax.nn.silu(h @ w_gate) * (h @ w_up)) @ w_down

def second_inputs(seed: int = 0) -> dict:
    key = jax.random.key(seed)
    ks = jax.random.split(key, 20)
    f32 = jnp.float32

    def nrm(k, shape, scale):
        return jax.random.normal(k, shape, f32) * scale

    x = jax.random.normal(ks[0], (BATCH, SEQ, D_MODEL), f32)
    dt_init = jnp.exp(jax.random.uniform(ks[5], (DEPTH, SSD_HEADS), f32, np.log(1e-3), np.log(1e-1)))
    dt_bias = dt_init + jnp.log(-jnp.expm1(-dt_init))
    return {
        'x': x,
        'norm_mix_w': 1.0 + nrm(ks[1], (DEPTH, D_MODEL), 0.05),
        'w_in': nrm(ks[2], (DEPTH, D_MODEL, IN_DIM), D_MODEL ** -0.5),
        'ssd_conv_w': nrm(ks[3], (DEPTH, SSD_CONV, SSD_XBC), SSD_CONV ** -0.5),
        'ssd_conv_b': nrm(ks[4], (DEPTH, SSD_XBC), 0.01),
        'dt_bias': dt_bias,
        'a_log': jnp.log(jax.random.uniform(ks[6], (DEPTH, SSD_HEADS), f32, 1.0, 16.0)),
        'd_skip': 1.0 + nrm(ks[7], (DEPTH, SSD_HEADS), 0.1),
        'ssd_norm_w': 1.0 + nrm(ks[8], (DEPTH, SSD_INNER), 0.05),
        'w_ssd_proj': nrm(ks[9], (DEPTH, SSD_INNER, D_MODEL), SSD_INNER ** -0.5),
        'sconv_w': nrm(ks[10], (DEPTH, SCONV_K, SCONV_DIM), SCONV_K ** -0.5),
        'w_sconv_proj': nrm(ks[11], (DEPTH, SCONV_DIM, D_MODEL), SCONV_DIM ** -0.5),
        'w_o': nrm(ks[12], (DEPTH, D_MODEL, D_MODEL), D_MODEL ** -0.5),
        'norm_ffn_w': 1.0 + nrm(ks[13], (DEPTH, D_MODEL), 0.05),
        'w_gate': nrm(ks[14], (DEPTH, D_MODEL, FFN_HIDDEN), D_MODEL ** -0.5),
        'w_up': nrm(ks[15], (DEPTH, D_MODEL, FFN_HIDDEN), D_MODEL ** -0.5),
        'w_down': nrm(ks[16], (DEPTH, FFN_HIDDEN, D_MODEL), FFN_HIDDEN ** -0.5),
        'final_norm_w': 1.0 + nrm(ks[17], (D_MODEL,), 0.05),
    }

def second_block(x, norm_mix_w, w_in, ssd_conv_w, ssd_conv_b, dt_bias, a_log, d_skip, ssd_norm_w,
              w_ssd_proj, sconv_w, w_sconv_proj, w_o, norm_ffn_w, w_gate, w_up, w_down,
              final_norm_w):
    h = x
    for i in range(DEPTH):
        h = h + hybrid_mixer(rmsnorm_2(h, norm_mix_w[i]), w_in[i], ssd_conv_w[i], ssd_conv_b[i],
                             dt_bias[i], a_log[i], d_skip[i], ssd_norm_w[i], w_ssd_proj[i],
                             sconv_w[i], w_sconv_proj[i], w_o[i])
        h = h + swiglu(rmsnorm_2(h, norm_ffn_w[i]), w_gate[i], w_up[i], w_down[i])
    return rmsnorm_2(h, final_norm_w)


def setup_inputs(seed=0):
    out = dict(first_inputs(seed))
    for name, value in second_inputs(seed + 1).items():
        if name != "x":
            out[name + "_2"] = value
    return out


def reference(
    x, c, w_cond, b_cond, g_mix_pre, g_mix_post, w_in, w_pool, pool_scale, w_out, g_ffn_pre,
    g_ffn_post, w_gate, w_up, w_down, norm_mix_w_2, w_in_2, ssd_conv_w_2, ssd_conv_b_2,
    dt_bias_2, a_log_2, d_skip_2, ssd_norm_w_2, w_ssd_proj_2, sconv_w_2, w_sconv_proj_2, w_o_2,
    norm_ffn_w_2, w_gate_2, w_up_2, w_down_2, final_norm_w_2,
):
    x = first_block(
        x, c, w_cond, b_cond, g_mix_pre, g_mix_post, w_in, w_pool, pool_scale, w_out, g_ffn_pre,
        g_ffn_post, w_gate, w_up, w_down,
    )
    return second_block(
        x, norm_mix_w_2, w_in_2, ssd_conv_w_2, ssd_conv_b_2, dt_bias_2, a_log_2, d_skip_2,
        ssd_norm_w_2, w_ssd_proj_2, sconv_w_2, w_sconv_proj_2, w_o_2, norm_ffn_w_2, w_gate_2,
        w_up_2, w_down_2, final_norm_w_2,
    )


_drawn_inputs = setup_inputs


def setup_inputs(seed=0):
    import zlib

    import numpy as np

    out = dict(_drawn_inputs(seed))
    spreads = {}
    factors = {'b_cond': 2.863, 'ssd_conv_b_2': 8.0, 'ssd_norm_w_2': 2.842, 'norm_ffn_w_2': 2.799}
    for name, (base, spread) in spreads.items():
        noise = np.random.default_rng([zlib.crc32(name.encode()), seed]).standard_normal(out[name].shape)
        drawn = base * np.exp(spread * noise) if base else spread * noise
        out[name] = __import__('jax').numpy.asarray(drawn.astype(out[name].dtype))
    for name, factor in factors.items():
        out[name] = (out[name] * factor).astype(out[name].dtype)
    return out
```

```python
from contextlib import ExitStack

import concourse.bass as bass
from concourse import mybir

F32 = mybir.dt.float32
F32R = mybir.dt.float32r
ALU = mybir.AluOpType
ACT = mybir.ActivationFunctionType

P = 128
T = 512
D = 1024
KT = D // P
FT = 2816 // P
NCH = T // P
EPS = 1e-6
RING = 4
R0 = 4
LEAD = 3

HEADS = 8
KEYS = [(0, 0), (1, 512), (3, 896), (2, 1024)]
KCOL = dict(KEYS)
NZ = 1280
PARTS = [(T, NZ - T, [(1, 512), (3, 896), (2, 1024)]), (0, T, [(0, 0)])]

GROUPS = 4
DOWN_K = [(0, 6), (6, 6), (12, 5), (17, 5)]

U_IN, U_OUT, U_GU1, U_DN1 = 0, 16, 24, 68
U_SC, U_SCP, U_BC, U_SSD, U_MRG, U_WO = 100, 124, 140, 148, 180, 204
U_GU2, U_DN2, U_END = 212, 256, 288

_VECS = [("c", 8), ("b_cond", 48), ("g_mix_pre", 8), ("g_mix_post", 8), ("g_ffn_pre", 8), ("g_ffn_post", 8),
         ("pool_scale", 4), ("norm_mix_w_2", 8), ("conv_w", 96), ("conv_b", 24), ("ssd_norm_w_2", 16),
         ("sconv_w", 24), ("norm_ffn_w_2", 8), ("final_norm_w_2", 8), ("d_skip", 16), ("dt_bias", 32),
         ("a_log", 32), ("eps", 1)]
V, NV = {}, 0
for _n, _k in _VECS:
    V[_n] = NV
    NV += _k

_CONS = [("ones", 128), ("after", 128), ("upto", 128), ("ident", 128), ("inv", 64)]
NSEL = 12 * P
C, NC = {}, 0
for _n, _k in _CONS:
    C[_n] = NC
    NC += _k


def hybrid_blocks(nc, w8, w22, wcond, wdt, wpool, vecs, cons, atts, sels, xin, out):
    ctx = ExitStack()

    def sb(name, shape, dt=F32, stack=ctx):
        return stack.enter_context(nc.sbuf_tensor(name, shape, dt))

    def sem(name):
        return ctx.enter_context(nc.semaphore(name))

    with ctx:
        con = sb("con", [P, NC])
        with ExitStack() as over:
            sel_raw = sb("sel_raw", [40, NSEL], F32, over)
        sel = sb("sel", [40, NSEL], F32R)
        vec = sb("vec", [P, NV])
        x = sb("x", [P, KT, T])
        raw = sb("raw", [P, RING, 1024])
        whi = sb("whi", [P, RING, 1024], F32R)
        wlo = sb("wlo", [P, RING, 1024], F32R)
        rr = sb("rr", [P, T])
        sq = sb("sq", [P, 2, T])
        ssum = sb("ssum", [P, T])
        cvec = sb("cvec", [P, KT])
        mod = sb("mod", [P, 48])
        amix = sb("amix", [P, KT])
        gmix = sb("gmix", [P, KT])
        affn = sb("affn", [P, KT])
        gffn = sb("gffn", [P, KT])
        halves = sb("halves", [P, 32])
        wdtr = sb("wdtr", [P, KT, 32])

        def region(build):
            with ExitStack() as s:
                return build(lambda name, shape, dt=F32, stack=s: sb(name, shape, dt, stack))

        def phase_a(a):
            t = dict(mixh=a("mixh", [P, KT, T], F32R), mixl=a("mixl", [P, KT, T], F32R),
                     h1h=a("h1h", [P, KT, T], F32R), h1l=a("h1l", [P, KT, T], F32R), cond=a("cond", [P, RING, 1024]),
                     macc=a("macc", [P, 2, 1024]),
                     att=a("att", [P, 4, P]), late=a("late", [P, 2, P], F32R))
            with ExitStack() as s:
                t.update(mix1=a("mix1", [P, KT, T], F32, s))
            t.update(qT=a("qT", [P, 2, T]), kT=a("kT", [P, 2, T]), vT=a("vT", [P, T]), vtok=a("vtok", [P, 2, NCH, P]),
                     az=a("az", [P, NZ]), sp_=a("sp", [P, NZ]), pw=a("pw", [P, NZ]),
                     padA=a("padA", [P, 16 + T]), padB=a("padB", [P, 16 + T]), padC=a("padC", [P, 16 + T]),
                     pooled=a("pooled", [P, T]), wp=a("wp", [P, 4, P]), ht1=a("ht1", [P, 2, T]),
                     pfix=a("pfix", [P, 16]))
            return t.values()
        (mixh, mixl, h1h, h1l, cond, macc, att, late, mix1, qT, kT, vT, vtok, az, sp_, pw, padA, padB, padC, pooled, wp,
         ht1, pfix) = region(phase_a)

        def phase_f(n):
            def build(a):
                fh, fl = a(f"fh{n}", [P, FT, T], F32R), a(f"fl{n}", [P, FT, T], F32R)
                with ExitStack() as s:
                    mix = a(f"mixf{n}", [P, KT, T], F32, s)
                return (fh, fl, mix, a(f"hf{n}h", [P, KT, T], F32R), a(f"hf{n}l", [P, KT, T], F32R),
                        a(f"htf{n}", [P, 2, T]), a(f"sg{n}", [P, 2, T]), a(f"ff{n}", [P, 2, T]))
            return build
        fh1, fl1, mix2, h2h, h2l, ht2, sg1, ff1 = region(phase_f(1))
        fh2, fl2, outT, h4h, h4l, ht4, sg2, ff2 = region(phase_f(2))

        def phase_e(a):
            t = dict(h3h=a("h3h", [P, KT, T], F32R), h3l=a("h3l", [P, KT, T], F32R))
            with ExitStack() as s:
                t.update(ml=a("ml", [P, KT, T], F32R, s))
            t.update(mrg=a("mrg", [P, KT, T]))
            with ExitStack() as s:
                t.update(vh=a("vh", [P, KT, T], F32R, s), vl=a("vl", [P, KT, T], F32R, s), ht3=a("ht3", [P, 2, T], F32, s),
                         cb=a("cb", [P, 2, T], F32, s), pr=a("pr", [P, 2, 2 + T], F32, s), cv=a("cv", [P, 2, T], F32, s),
                         sgb=a("sgb", [P, 2, T], F32, s))
            with ExitStack() as s:
                t.update(mh=a("mh", [P, KT, T], F32R, s))
            t.update(bc=a("bc", [P, 8, T]))
            with ExitStack() as s:
                a("beside_vl", [P, KT, T], F32, s)
                t.update(wdth=a("wdth", [P, KT, 32], F32R, s),
                         wdtl=a("wdtl", [P, KT, 32], F32R, s))
            with ExitStack() as s:
                t.update(yl=a("yl", [P, 16, T], F32R, s), yh=a("yh", [P, 16, T], F32R, s),
                         sga=a("sga", [P, 2, T], F32, s), ta=a("ta", [P, 2, T], F32, s))
            t.update(yy=a("yy", [P, 16, T]))
            t.update(bt=a("bt", [P, T]), ct=a("ct", [P, T]), dag=a("dag", [P, NCH, 8]))
            t.update(dt=a("dt", [P, NCH, 32]), dte=a("dte", [P, NCH, 32]), da=a("da", [P, NCH, 32]),
                     dta=a("dta", [P, NCH, 32]), ea=a("ea", [P, 32]),
                     atok=a("atok", [P, NCH, 32]), toend=a("toend", [P, NCH, 32]), dec=a("dec", [P, NCH, 32]),
                     cbm=a("cbm", [P, NCH, P]),
                     btok=a("btok", [P, NCH, P]), atg=a("atg", [40, T], F32R),
                     xr=a("xr", [P, 2, 3 + T]), cx=a("cx", [P, 2, T]), th=a("th", [P, T]), xs=a("xs", [P, 2, T]),
                     xdt=a("xdt", [P, NCH, P]), xde=a("xde", [P, 3, P]), seg=a("seg", [P, 2, NCH, P]),
                     st=a("st", [P, 3, P]), eab=a("eab", [P, T]), yb=a("yb", [P, T]), gz=a("gz", [P, T]))
            return t.values()
        (h3h, h3l, ml, mrg, vh, vl, ht3, cb, pr, cv, sgb, mh, bc, wdth, wdtl, yl, yh, sga, ta, yy, bt, ct, dag, dt, dte, da,
         dta, ea, atok, toend, dec, cbm, btok, atg, xr, cx, th, xs, xdt, xde, seg, st, eab, yb,
         gz) = region(phase_e)

        PR = ctx.enter_context(nc.psum_tensor("PR", [P, 4, T], F32))
        AX = ctx.enter_context(nc.psum_tensor("AX", [P, 4, T], F32))
        AXf = AX[:, :, :].rearrange("p a b -> p (a b)")

        raw_in = [sem(f"raw_in{j}") for j in range(RING)]
        cond_in = [sem(f"cond_in{j}") for j in range(RING)]
        s_con, s_x, s_wdt, s_out, out_ready = map(sem, ("s_con", "s_x", "s_wdt", "s_out", "out_ready"))
        hi_ready, lo_ready, unit_used, cond_used = map(sem, ("hi_ready", "lo_ready", "unit_used", "cond_used"))
        cvec_ready, mod_ready, msum_done = map(sem, ("cvec_ready", "mod_ready", "msum_done"))
        sq_ready, sq_used, ss_ready, ln_ready, r_ready = map(sem, ("sq_ready", "sq_used", "ss_ready", "ln_ready", "r_ready"))
        msq_ready, vacc = map(sem, ("msq_ready", "vacc"))
        hs_ready, ht_ready, hh_ready, hl_ready, upd_ready, res_ready = map(
            sem, ("hs_ready", "ht_ready", "hh_ready", "hl_ready", "upd_ready", "res_ready"))
        qkvu_ready, vtr_done, vtok_ready = map(sem, ("qkvu_ready", "vtr_done", "vtok_ready"))
        late_ready, z_done, az_ready, e_ready, l_ready, sp_ready = map(
            sem, ("late_ready", "z_done", "az_ready", "e_ready", "l_ready", "sp_ready"))
        cum_done, w_ready, pv_done, mixh_ready, mixl_ready = map(
            sem, ("cum_done", "w_ready", "pv_done", "mixh_ready", "mixl_ready"))
        pad_zero, pstep, pooled_ready, pooly_done, poolh_ready, pooll_ready = map(
            sem, ("pad_zero", "pstep", "pooled_ready", "pooly_done", "poolh_ready", "pooll_ready"))
        mix_ready, sg_ready, ff_ready, fh_ready, fl_ready = map(
            sem, ("mix_ready", "sg_ready", "ff_ready", "fh_ready", "fl_ready"))
        c_ready, pr_ready, cstep, cv_ready, vh_ready, vl_ready, sgb_ready, mrg_ready = map(
            sem, ("c_ready", "pr_ready", "cstep", "cv_ready", "vh_ready", "vl_ready", "sgb_ready", "mrg_ready"))
        xr_ready, tap, conv_ready, bc_ready, dt_done, dt_v, dt_a, acum_done, atok_ready = map(
            sem, ("xr_ready", "tap", "conv_ready", "bc_ready", "dt_done", "dt_v", "dt_a", "acum_done", "atok_ready"))
        grp_ready, cb_done, btr_done, atg_done, cbm_ready, btok_ready, atg_ready, atgl_ready, sel_ready = map(
            sem, ("grp_ready", "cb_done", "btr_done", "atg_done", "cbm_ready", "btok_ready", "atg_ready", "atgl_ready",
                  "sel_ready"))
        th_ready, xs_ready, xtr_done, xdt_ready, xde_ready, abc_done, seg_ready, ex_ready, sc_ready = map(
            sem, ("th_ready", "xs_ready", "xtr_done", "xdt_ready", "xde_ready", "abc_done", "seg_ready", "ex_ready",
                  "sc_ready"))
        pair_done, eab_ready, stp_done, st_step, y_done, yb_ready, yo_ready, y2_ready = map(
            sem, ("pair_done", "eab_ready", "stp_done", "st_step", "y_done", "yb_ready", "yo_ready", "y2_ready"))
        thz_ready, sz_ready, yv_ready, vsq_ready, yy_ready = map(
            sem, ("thz_ready", "sz_ready", "yv_ready", "vsq_ready", "yy_ready"))
        yh_ready, yl_ready, sga_ready, ta_ready, mh_ready, ml_ready = map(
            sem, ("yh_ready", "yl_ready", "sga_ready", "ta_ready", "mh_ready", "ml_ready"))

        block = ctx.enter_context(nc.Block())

        def con_(name, lo=0, n=P, rows=P):
            return con[0:rows, C[name] + lo:C[name] + lo + n]

        def vec_(name, k):
            return vec[:, bass.ds(k + V[name], 1)]

        def tile(t, k):
            return t[:, bass.ds(k, 1), :].rearrange("p a b -> p (a b)")

        def spread(ap, shape):
            return ap.unsqueeze(len(ap.shape)).broadcast_to(shape)

        @block.sync
        def _(sp):
            def load_unit(u, j, src):
                if not isinstance(u, int) or u >= RING:
                    sp.wait_ge(lo_ready, u - (RING - 1))
                sp.dma_start(raw[:, j, 0:src.shape[-1]], src).then_inc(raw_in[j], 16)

            def load_cond(n, j):
                if not isinstance(n, int) or n >= RING:
                    sp.wait_ge(cond_used, n - (RING - 1))
                sp.dma_start(cond[:, j, :], wcond[bass.ds(n, 1), :, :].rearrange("a p n -> (a p) n")).then_inc(
                    cond_in[j], 16)

            def w8_at(u):
                return w8[bass.ds(u, 1), :, :].rearrange("a p n -> (a p) n")

            def stream(first, end, at=0):
                with sp.Fori(0, (end - first) // RING) as i:
                    for j in range(RING):
                        load_unit(RING * i + (first + j), j, w8_at(RING * i + (first + j - at)))

            def down(first, block0):
                with sp.Fori(0, KT) as i:
                    for j, (k0, n) in enumerate(DOWN_K):
                        load_unit(RING * i + (first + j), j,
                                  w22[bass.ds(i + block0, 1), :, k0 * P:(k0 + n) * P].rearrange("a p n -> (a p) n"))

            sp.dma_start(vec[:, :], vecs[:, :]).then_inc(s_con, 16)
            sp.dma_start(x[:, :, :], xin[:, :, :]).then_inc(s_x, 16)
            sp.dma_start(con[:, :], cons[:, :]).then_inc(s_con, 16)
            sp.dma_start(att[:, :, :], atts[:, :, :]).then_inc(s_con, 16)
            for n in range(RING):
                load_cond(n, n)
            with sp.Fori(0, 2) as i:
                for j in range(RING):
                    load_cond(RING * i + (RING + j), j)
            load_unit(0, 0, w8_at(0))
            for n in range(12, 16):
                load_cond(n, n % RING)
            for u in range(1, RING):
                load_unit(u, u, w8_at(u))
            sp.dma_start(wp[:, :, :], wpool[:, :, :]).then_inc(s_con, 16)
            sp.dma_start(sel_raw[:, :], sels[:, :]).then_inc(s_con, 16)
            sp.dma_start(wdtr[:, :, :], wdt[:, :, :]).then_inc(s_wdt, 16)
            for j in range(RING):
                load_unit(RING + j, j, w8_at(RING + j))
            for j in range(RING):
                load_cond(16 + j, j)

            def for_head(i, e):
                for j in (2 * e, 2 * e + 1):
                    load_unit(4 * i + (8 + j), j, w8_at(4 * i + (8 + j)))
                for j in range(RING):
                    load_cond(8 * i + (20 + 4 * e + j), j)

            with sp.Fori(0, 3) as i:
                for_head(i, 0)
                for_head(i, 1)
            for_head(3, 0)
            for u in (22, 23):
                load_unit(u, u % RING, w8_at(u))
            stream(U_GU1, U_DN1)
            down(U_DN1, 0)
            stream(U_SC, U_DN2, 32)
            down(U_DN2, KT)
            for k in range(KT):
                sp.wait_ge(out_ready, k + 1)
                sp.dma_start(out[:, k, :], outT[:, k, :]).then_inc(s_out, 16)
            sp.wait_ge(s_out, 16 * KT)

        @block.gpsimd
        def _(pool):
            with pool.Fori(0, U_END // RING) as i:
                for j in range(RING):
                    pool.wait_ge(hi_ready, RING * i + (j + 1))
                    pool.tensor_tensor(wlo[:, j, :], raw[:, j, :], whi[:, j, :], ALU.subtract).then_inc(lo_ready, 1)

        @block.tensor
        def _(pe):
            def banks(readers, nb=4):
                n = len(readers)

                def wait(i, j):
                    it, pos = (i, j - nb) if j >= nb else (i - 1, j - nb + n)
                    s, base = readers[pos]
                    each = sum(r[0] is s for r in readers)
                    upto = sum(r[0] is s for r in readers[:pos + 1])
                    if j >= nb:
                        pe.wait_ge(s, i * each + (base + upto))
                    else:
                        pe.wait_ge(s, i * each + (base + upto - each))
                return wait

            def unit(u, j, oh, ol, k0, n, bank, first=True, last=True, each=None, halfway=None):
                pe.wait_ge(lo_ready, u + 1)
                for k in range(n):
                    if each is not None:
                        pe.wait_ge(*each(k))
                    if k == n // 2 and halfway is not None:
                        halfway()
                    w = slice(k * P, (k + 1) * P)
                    pe.matmul(bank, whi[:, j, w], oh[:, k0 + k, :], start=first and k == 0, stop=False)
                    pe.matmul(bank, whi[:, j, w], ol[:, k0 + k, :], start=False, stop=False)
                    mm = pe.matmul(bank, wlo[:, j, w], oh[:, k0 + k, :], start=False, stop=last and k == n - 1)
                mm.then_inc(unit_used, 1)

            def sumsq(first):
                for k in range(KT):
                    pe.wait_ge(sq_ready, first + k + 1)
                    mm = pe.matmul(AX[:, 0, :], con_("ones"), sq[:, k % 2, :], start=k == 0, stop=k == KT - 1)
                    mm.then_inc(sq_used, 1)

            def sum_once(n):
                pe.wait_ge(vacc, n)
                pe.matmul(AX[:, 0, :], con_("ones"), ssum[:, :], start=True, stop=True).then_inc(ss_ready, 1)

            def mod_sum(m):
                pe.wait_ge(cond_used, KT * (m + 1))
                if m == 2:
                    pe.wait_ge(mod_ready, 1)
                for k in range(KT):
                    mm = pe.matmul(PR[:, 3, KT * m + k:KT * m + k + 1], macc[:, m % 2, k * P:(k + 1) * P],
                                   con_("ones", 0, 1), start=True, stop=True)
                mm.then_inc(msum_done, 1)

            pe.wait_ge(s_con, 48)
            sumsq(0)
            mod_sum(0)
            mod_sum(1)

            def in_unit(u):
                if u >= 2:
                    pe.wait_ge(qkvu_ready, u - 1)
                unit(u, u % RING, h1h, h1l, 0, KT, PR[:, u % 2, :],
                     each=(lambda k: (hl_ready, k + 1)) if u == 0 else None)

            def v_turn(p):
                pe.wait_ge(qkvu_ready, 4 * p + 3)
                if p >= 1:
                    pe.wait_ge(pooll_ready, p)
                for c in range(NCH):
                    mm = pe.transpose(PR[:, 2, c * P:(c + 1) * P], vT[:, c * P:(c + 1) * P], con_("ident"))
                mm.then_inc(vtr_done, 1)

            def scores(h):
                p, r = h // 2, slice(64 * (h % 2), 64 * (h % 2) + 64)
                pe.wait_ge(qkvu_ready, 4 * p + 2)
                if h == 0:
                    pe.wait_ge(mod_ready, 1)
                    pe.wait_ge(late_ready, 1)
                for n, (_, _, blocks) in enumerate(PARTS):
                    if h >= 1:
                        pe.wait_ge(w_ready, 2 * h - 1 + n)
                    for j, c in blocks:
                        pe.matmul(AXf[:, c:c + T - j * P], kT[r, p % 2, j * P:(j + 1) * P], qT[r, p % 2, j * P:T],
                                  start=j != 3, stop=False, skip_group_check=True)
                    for j, c in blocks:
                        mm = pe.matmul(AXf[:, c:c + P], late[:, 0, :], late[:, 1, :], start=False, stop=False,
                                       skip_group_check=True)
                    mm.then_inc(z_done, 1)

            def later_keys(h):
                for n, (_, _, blocks) in enumerate(PARTS):
                    pe.wait_ge(sp_ready, 2 * h + n + 1)
                    for j, c in blocks:
                        mm = pe.matmul(AXf[:, c:c + T - j * P], att[:, 2, :], sp_[:, c:c + T - j * P],
                                       start=False, stop=j == NCH - 1, skip_group_check=True)
                        for j2 in range(j + 1, NCH):
                            c2, off = KCOL[j2], c + (j2 - j) * P
                            mm = pe.matmul(AXf[:, off:off + T - j2 * P], att[:, 3, :], sp_[:, c2:c2 + T - j2 * P],
                                           start=False, stop=j2 == NCH - 1, skip_group_check=True)
                    mm.then_inc(cum_done, 1)

            def values(h):
                p, e = h // 2, h % 2
                pe.wait_ge(w_ready, 2 * h + 2)
                pe.wait_ge(vtok_ready, p + 1)
                if e == 0 and p >= 1:
                    pe.wait_ge(mixl_ready, p)
                for j in range(NCH):
                    c = KCOL[j]
                    mm = pe.matmul(AX[64 * e:64 * e + 64, 3, j * P:T], vtok[:, p % 2, j, 64 * e:64 * e + 64],
                                   pw[:, c:c + T - j * P], start=j == 0, stop=j == NCH - 1, skip_group_check=True)
                mm.then_inc(pv_done, 1)

            def pool_map(g):
                pe.wait_ge(pooled_ready, g + 1)
                if g == 0:
                    pe.wait_ge(s_con, 80)
                pe.wait_ge(vtok_ready, g + 1)
                pe.matmul(PR[:, 2, :], wp[:, g, :], pooled[:, :], start=True, stop=True).then_inc(pooly_done, 1)

            for u in range(4):
                in_unit(u)
            v_turn(0)
            for h in range(HEADS):
                p, e = h // 2, h % 2
                scores(h)
                if p < 3:
                    in_unit(4 * (p + 1) + 2 * e)
                later_keys(h)
                if p < 3:
                    in_unit(4 * (p + 1) + 2 * e + 1)
                if e == 0:
                    pool_map(p)
                else:
                    mod_sum(2 + p)
                values(h)
                if e == 1 and p < 3:
                    v_turn(p + 1)

            pe.wait_ge(mixl_ready, 4)
            pe.wait_ge(pooll_ready, 4)
            pe.wait_ge(mod_ready, 3)
            wait = banks([(mix_ready, R0)] * 4)
            with pe.Fori(0, 2) as i:
                for j in range(4):
                    wait(i, j)
                    unit(4 * i + (U_OUT + j), j, mixh, mixl, 0, KT, PR[:, j, :])
            sum_once(9)
            sumsq(8)

            def feed_forward(n, first_u, first_dn, hh, hl, hl0, fh, fl, down_reader):
                wait = banks([(sg_ready, R0 + FT * (n - 1)), (ff_ready, R0 + FT * (n - 1))] * 2)
                with pe.Fori(0, FT // 2) as i:
                    for j in range(4):
                        wait(i, j)
                        unit(4 * i + (first_u + j), j, hh, hl, 0, KT, PR[:, j, :],
                             each=(lambda k: (hl_ready, hl0 + k + 1)) if j == 0 else None)
                pe.wait_ge(sg_ready, R0 + FT * n - 1)
                pe.wait_ge(ff_ready, R0 + FT * n - 1)
                wait = banks([down_reader] * 2, nb=2)
                with pe.Fori(0, KT // 2) as i:
                    for b in range(2):
                        wait(i, b)
                        for j, (k0, nk) in enumerate(DOWN_K):
                            if b == 0:
                                pe.wait_ge(fl_ready, FT * (n - 1) + k0 + nk)
                            unit(8 * i + (first_dn + 4 * b + j), j, fh, fl, k0, nk, PR[:, b, :],
                                 first=j == 0, last=j == 3)

            pe.wait_ge(mix_ready, R0 + 8)
            feed_forward(1, U_GU1, U_DN1, h2h, h2l, 8, fh1, fl1, (mix_ready, R0 + 8))
            sum_once(18)
            sumsq(16)

            wait = banks([(c_ready, R0), (pr_ready, R0), (cv_ready, R0)] * 4)
            with pe.Fori(0, 2) as i:
                for j in range(12):
                    wait(i, j)
                    unit(12 * i + (U_SC + j), j % 4, h3h, h3l, 0, KT, PR[:, j % 4, :],
                         each=(lambda k: (hl_ready, 17 + k)) if j == 0 else None)
            pe.wait_ge(cv_ready, R0 + 7)
            wait = banks([(sgb_ready, R0), (mrg_ready, R0)] * 2)
            with pe.Fori(0, 4) as i:
                for j in range(4):
                    wait(i, j)
                    if j == 1:
                        pe.wait_ge(vl_ready, KT)
                    oh, ol = (h3h, h3l) if j % 2 == 0 else (vh, vl)
                    unit(4 * i + (U_SCP + j), j, oh, ol, 0, KT, PR[:, j, :])

            pe.wait_ge(dt_v, 1)
            for c in range(NCH):
                for k in range(KT):
                    for n, (hx, wx) in enumerate(((h3h, wdth), (h3l, wdth), (h3h, wdtl))):
                        mm = pe.matmul(AX[:, 0, 32 * c:32 * c + 32], hx[:, k, c * P:(c + 1) * P], wx[:, k, :],
                                       start=k == 0 and n == 0, stop=k == KT - 1 and n == 2)
            mm.then_inc(dt_done, 1)
            pe.wait_ge(sgb_ready, R0 + 7)
            wait = banks([(xr_ready, R0)] * 4)
            with pe.Fori(0, 2) as i:
                for j in range(4):
                    wait(i, j)
                    if j == 1:
                        pe.wait_ge(mrg_ready, R0 + KT)
                    unit(4 * i + (U_BC + j), j, h3h, h3l, 0, KT, PR[:, j, :])
            pe.wait_ge(dt_v, 6)
            for n, m in enumerate(("upto", "after", "ones")):
                mm = pe.matmul(AX[:, 1, n * P:(n + 1) * P], con_(m), da[:, :, :].rearrange("p c h -> p (c h)"),
                               start=True, stop=True)
            mm.then_inc(acum_done, 1)

            def ssd_first(g, j):
                pe.wait_ge(xs_ready, 4 * g + (j + 1))
                pe.wait_ge(btok_ready, g + 1)
                if j > 0:
                    pe.wait_ge(yo_ready, 4 * g + j)
                for c in range(NCH):
                    mm = pe.transpose(AX[:, 3, c * P:(c + 1) * P], xs[:, j % 2, c * P:(c + 1) * P], con_("ident"))
                mm.then_inc(xtr_done, 1)
                pe.wait_ge(atgl_ready, g + 1)
                if j > 0 or not isinstance(g, int):
                    pe.wait_ge(eab_ready, 4 * g + j)
                if j == 1 and not isinstance(g, int):
                    pe.wait_ge(ln_ready, g + 5)
                for e in range(2):
                    pe.matmul(AX[:, e, :], sel[:, (2 * j + e) * P:(2 * j + e + 1) * P], atg[:, :], start=True, stop=True).then_inc(
                        abc_done, 1)

            def ssd_states(g, j):
                pe.wait_ge(xde_ready, 4 * g + (j + 1))
                for c in range(3):
                    mm = pe.matmul(AX[:, 3, c * P:(c + 1) * P], btok[:, c, :], xde[:, c, :], start=True, stop=True)
                mm.then_inc(stp_done, 1)
                pe.wait_ge(seg_ready, 8 * g + (2 * j + 1))
                pe.matmul(AX[:, 0, :], sel[:, (8 + j % 4) * P:(9 + j % 4) * P], atg[:, :], start=True, stop=True).then_inc(pair_done, 1)

            def ssd_second(g, j):
                if j != 0:
                    pe.wait_ge(yb_ready, 4 * g + j)
                for e in range(2):
                    pe.wait_ge(sc_ready, 8 * g + (2 * j + e + 1))
                    for c in range(NCH):
                        pe.matmul(AX[64 * e:64 * e + 64, 2, c * P:(c + 1) * P], xdt[:, c, 64 * e:64 * e + 64],
                                  seg[:, e, c, :], start=True, stop=True, skip_group_check=True)
                pe.wait_ge(st_step, 20 * g + 5 * (j + 1))
                for c in range(1, NCH):
                    mm = pe.matmul(AX[:, 3, c * P:(c + 1) * P], st[:, c - 1, :], ct[:, c * P:(c + 1) * P],
                                   start=True, stop=True)
                mm.then_inc(y_done, 1)

            wait = banks([(xr_ready, R0 + 8), (sz_ready, R0)] * 4)

            def group_sum(g):
                pe.wait_ge(vacc, 4 * g + 18)
                pe.matmul(AX[:, 1, :], con_("ones"), ssum[:, :], start=True, stop=True).then_inc(ss_ready, 1)

            def group_decays(g):
                pe.wait_ge(grp_ready, 3 * g + 2)
                pe.wait_ge(seg_ready, 8 * g) if not isinstance(g, int) else pe.wait_ge(atok_ready, 3)
                for c in range(NCH):
                    mm = pe.matmul(AX[0:8, 1, c * P:(c + 1) * P], dag[:, c, :], con_("upto"), start=True, stop=True,
                                   skip_group_check=True)
                mm.then_inc(atg_done, 1)

            def ssd_group(g):
                later = not isinstance(g, int)
                for j in range(4):
                    for q in range(2):
                        r = 2 * j + q
                        wait(g, r)
                        before = q == 0 and (j > 0 or later)

                        def halfway():
                            ssd_states(g, j - 1)
                            if j == 1 and later:
                                pe.wait_ge(seg_ready, 8 * g + 2)
                                group_sum(g)
                        unit(8 * g + (U_SSD + r), r % 4, h3h, h3l, 0, KT, PR[:, r % 4, :],
                             halfway=halfway if before else None)
                        if before:
                            ssd_second(g, j - 1)
                        if r == (0 if later else 1):
                            group_decays(g)
                    if j == 0:
                        pe.wait_ge(grp_ready, 3 * g + 3)
                        if later:
                            pe.wait_ge(yb_ready, 4 * g)
                        for c in range(NCH):
                            s = slice(c * P, (c + 1) * P)
                            mm = pe.matmul(AX[:, 2, s], bt[:, s], ct[:, s], start=True, stop=True)
                        mm.then_inc(cb_done, 1)
                        if later:
                            pe.wait_ge(yo_ready, 4 * g)
                        for c in range(NCH):
                            s = slice(c * P, (c + 1) * P)
                            mm = pe.transpose(AX[:, 3, s], bt[:, s], con_("ident"))
                        mm.then_inc(btr_done, 1)
                    ssd_first(g, j)
                    if j == 0:
                        pe.wait_ge(cbm_ready, g + 1)

            pe.wait_ge(sel_ready, 1)
            ssd_group(0)
            with pe.Fori(1, GROUPS) as g:
                ssd_group(g)

            wait = banks([(sga_ready, R0), (ta_ready, R0)] * 4)

            def merge(i, m, last_tile=False):
                wait(i, 2 * m)
                unit(12 * i + (U_MRG + 3 * m), (3 * m) % 4, h3h, h3l, 0, KT, PR[:, (2 * m) % 4, :],
                     halfway=(lambda: ssd_states(GROUPS, -1)) if last_tile else None)
                if last_tile:
                    ssd_second(GROUPS, -1)
                    pe.wait_ge(seg_ready, 8 * GROUPS)
                    group_sum(GROUPS)
                    pe.wait_ge(sz_ready, R0 + 16)
                wait(i, 2 * m + 1)
                for q in range(2):
                    unit(12 * i + (U_MRG + 3 * m + 1 + q), (3 * m + 1 + q) % 4, yh, yl, KT * q, KT,
                         PR[:, (2 * m + 1) % 4, :], first=q == 0, last=q == 1,
                         each=(lambda k: (yl_ready, KT * q + k + 1)) if last_tile else None)

            for m in range(8):
                merge(m // 4, m % 4, last_tile=m == 0)
            pe.wait_ge(ml_ready, KT)
            wait = banks([(res_ready, 16)] * 4)
            with pe.Fori(0, 2) as i:
                for j in range(4):
                    wait(i, j)
                    unit(4 * i + (U_WO + j), j, mh, ml, 0, KT, PR[:, j, :])
            sumsq(24)
            feed_forward(2, U_GU2, U_DN2, h4h, h4l, 24, fh2, fl2, (res_ready, 24))
            sumsq(32)

        @block.scalar
        def _(act):
            def hi(i, per, c):
                j = c % RING
                if not isinstance(i, int) or per * i + c >= RING:
                    act.wait_ge(unit_used, per * i + (c - RING + 1))
                act.wait_ge(raw_in[j], (per // RING * 16) * i + 16 * (c // RING + 1))
                act.activation(whi[:, j, :], raw[:, j, :], ACT.Copy).then_inc(hi_ready, 1)

            def squares(first, res0):
                for k in range(KT):
                    if first + k >= 2:
                        act.wait_ge(sq_used, first + k - 1)
                    if res0 is None:
                        act.wait_ge(s_x, 16)
                    else:
                        act.wait_ge(res_ready, res0 + k + 1)
                    act.activation(sq[:, k % 2, :], x[:, k, :], ACT.Square).then_inc(sq_ready, 1)

            def rms(n, ready, count, width=D, bank=0):
                act.preload_act_table_set("natural_log_exp_and_others")
                act.wait_ge(ready, count)
                act.activation(rr[:, :], AX[:, bank, :], ACT.Ln, bias=vec_("eps", 0), scale=1.0 / width).then_inc(ln_ready, 1)
                act.wait_ge(ln_ready, n)
                act.activation(rr[:, :], rr[:, :], ACT.Exp, scale=-0.5).then_inc(r_ready, 1)

            def split_h(first, ht, hh):
                for k in range(KT):
                    act.wait_ge(ht_ready, first + k + 1)
                    act.activation(hh[:, k, :], ht[:, k % 2, :], ACT.Copy).then_inc(hh_ready, 1)

            for s in (mix_ready, sg_ready, c_ready, sgb_ready, xr_ready, sga_ready):
                act.sem_inc(s, R0)

            act.wait_ge(s_con, 48)
            act.activation(cvec[:, :], vec[:, V["c"]:V["c"] + KT], ACT.Silu).then_inc(cvec_ready, 1)
            squares(0, None)
            act.activation(late[:, :, :], att[:, 0:2, :], ACT.Copy).then_inc(late_ready, 1)
            rms(1, sq_used, 8)
            for u in range(LEAD):
                hi(0, 4, u)
            split_h(0, ht1, h1h)

            def in_result(u):
                p, kind = u // 4, u % 4
                act.wait_ge(unit_used, u + 1)
                if kind == 0:
                    if p >= 2:
                        act.wait_ge(z_done, 4 * p - 4)
                    ins = act.activation(qT[:, p % 2, :], PR[:, u % 2, :], ACT.Copy, scale=0.125)
                elif kind == 1:
                    ins = act.activation(kT[:, p % 2, :], PR[:, u % 2, :], ACT.Copy)
                elif kind == 2:
                    if p >= 1:
                        act.wait_ge(vtr_done, p)
                    ins = act.activation(vT[:, :], PR[:, u % 2, :], ACT.Copy)
                else:
                    if p >= 1:
                        act.wait_ge(pooled_ready, p)
                    else:
                        act.wait_ge(pad_zero, 3)
                    ins = act.activation(padA[:, 16:], PR[:, u % 2, :], ACT.Copy)
                ins.then_inc(qkvu_ready, 1)

            def v_tok(p):
                act.wait_ge(vtr_done, p + 1)
                if p >= 2:
                    act.wait_ge(pv_done, 2 * p - 2)
                act.activation(vtok[:, p % 2, :, :].rearrange("p a b -> p (a b)"), PR[:, 2, :], ACT.Copy).then_inc(
                    vtok_ready, 1)

            def soft(h):
                for n, (c, w, _) in enumerate(PARTS):
                    k, cols = 2 * h + n + 1, slice(c, c + w)
                    act.wait_ge(z_done, k)
                    if h >= 1:
                        act.wait_ge(sp_ready, k - 2)
                    act.activation(az[:, cols], AXf[:, cols], ACT.Abs).then_inc(az_ready, 1)
                    act.wait_ge(az_ready, k)
                    act.activation(az[:, cols], az[:, cols], ACT.Exp, scale=-1.0).then_inc(e_ready, 1)
                    act.wait_ge(e_ready, k)
                    act.activation(az[:, cols], az[:, cols], ACT.Ln, bias=1.0).then_inc(l_ready, 1)

            def weights(h):
                for n, (c, w, _) in enumerate(PARTS):
                    act.wait_ge(cum_done, 2 * h + n + 1)
                    if h >= 1:
                        act.wait_ge(pv_done, h)
                    act.activation(pw[:, c:c + w], AXf[:, c:c + w], ACT.Exp).then_inc(w_ready, 1)

            def in_step(u):
                hi(0, 4, u + LEAD)
                in_result(u)

            for u in range(4):
                in_step(u)
            v_tok(0)
            for h in range(HEADS):
                p, e = h // 2, h % 2
                soft(h)
                if p < 3:
                    in_step(4 * (p + 1) + 2 * e)
                weights(h)
                if p < 3:
                    in_step(4 * (p + 1) + 2 * e + 1)
                if e == 0:
                    act.wait_ge(pooly_done, p + 1)
                    act.activation(mixh[:, 4 + p, :], PR[:, 2, :], ACT.Copy, scale=vec_("pool_scale", p)).then_inc(
                        poolh_ready, 1)
                else:
                    act.wait_ge(pv_done, h + 1)
                    act.activation(mixh[:, p, :], AX[:, 3, :], ACT.Copy).then_inc(mixh_ready, 1)
                    if p < 3:
                        v_tok(p + 1)

            def keep(sq_slot, bank, dst):
                act.activation(sq[:, sq_slot, :], bank, ACT.Square).then_inc(msq_ready, 1)
                act.activation(dst, bank, ACT.Copy).then_inc(mix_ready, 1)

            with act.Fori(0, 2) as i:
                for j in range(4):
                    hi(i, 4, U_OUT + j + LEAD)
                    act.wait_ge(unit_used, 4 * i + (U_OUT + j + 1))
                    act.wait_ge(vacc, 4 * i + (j + 1))
                    keep(j % 2, PR[:, j, :], tile(mix1, 4 * i + j))
            rms(2, ss_ready, 1)
            squares(8, 0)
            rms(3, sq_used, 16)
            split_h(8, ht2, h2h)

            def feed_forward(n, first_u, sg, ff, fh):
                with act.Fori(0, FT // 2) as i:
                    for b in range(2):
                        hi(i, 4, first_u + 2 * b + LEAD)
                        act.wait_ge(unit_used, 4 * i + (first_u + 2 * b + 1))
                        act.activation(sg[:, b, :], PR[:, 2 * b, :], ACT.Silu).then_inc(sg_ready, 1)
                        hi(i, 4, first_u + 2 * b + 1 + LEAD)
                        act.wait_ge(ff_ready, 2 * i + (R0 + FT * (n - 1) + b + 1))
                        act.activation(tile(fh, 2 * i + b), ff[:, b, :], ACT.Copy).then_inc(fh_ready, 1)

            feed_forward(1, U_GU1, sg1, ff1, fh1)
            with act.Fori(0, KT // 2) as i:
                for b in range(2):
                    for j in range(4):
                        hi(i, 8, U_DN1 + 4 * b + j + LEAD)
                    act.wait_ge(unit_used, 8 * i + (U_DN1 + 4 * b + 4))
                    act.wait_ge(vacc, 2 * i + (10 + b))
                    keep(b, PR[:, b, :], tile(mix2, 2 * i + b))
            rms(4, ss_ready, 2)
            squares(16, 8)
            rms(5, sq_used, 24)
            split_h(16, ht3, h3h)

            act.wait_ge(hl_ready, 24)
            act.wait_ge(s_wdt, 16)
            act.activation(wdth[:, :, :], wdtr[:, :, :], ACT.Copy).then_inc(dt_a, 1)
            with act.Fori(0, 2) as i:
                for m in range(4):
                    for q in range(3):
                        hi(i, 12, U_SC + 3 * m + q + LEAD)
                        if q == 0:
                            act.wait_ge(unit_used, 12 * i + (U_SC + 3 * m + 1))
                            act.activation(cb[:, m % 2, :], PR[:, (3 * m) % 4, :], ACT.Copy).then_inc(c_ready, 1)
                    act.wait_ge(cv_ready, 4 * i + (R0 + m + 1))
                    act.activation(tile(vh, 4 * i + m), cv[:, m % 2, :], ACT.Copy).then_inc(vh_ready, 1)
            with act.Fori(0, 4) as i:
                for j in range(4):
                    hi(i, 4, U_SCP + j + LEAD)
                    if j % 2 == 0:
                        act.wait_ge(unit_used, 4 * i + (U_SCP + j + 1))
                        act.wait_ge(mrg_ready, 2 * i + (R0 + j // 2 - 1))
                        act.activation(sgb[:, j // 2, :], PR[:, j, :], ACT.Sigmoid).then_inc(sgb_ready, 1)
            act.wait_ge(s_con, 80)
            act.activation(sel[:, :], sel_raw[:, :], ACT.Copy).then_inc(sel_ready, 1)
            act.activation(ea[:, :], vec[:, V["a_log"]:V["a_log"] + 32], ACT.Exp).then_inc(dt_a, 1)
            act.preload_act_table_set("natural_log_exp_and_others")
            act.wait_ge(dt_v, 4)
            act.activation(dte[:, :, :], dte[:, :, :], ACT.Exp).then_inc(dt_a, 1)
            act.wait_ge(dt_a, 3)
            act.activation(dte[:, :, :], dte[:, :, :], ACT.Ln, bias=1.0).then_inc(dt_a, 1)
            act.wait_ge(pad_zero, 5)
            with act.Fori(0, 2) as i:
                for j in range(4):
                    hi(i, 4, U_BC + j + LEAD)
                    act.wait_ge(unit_used, 4 * i + (U_BC + j + 1))
                    act.activation(xr[:, j % 2, 3:], PR[:, j, :], ACT.Copy).then_inc(xr_ready, 1)
                    act.wait_ge(conv_ready, 4 * i + (j + 1))
                    act.activation(tile(bc, 4 * i + j), cx[:, j % 2, :], ACT.Silu).then_inc(bc_ready, 1)
            act.wait_ge(acum_done, 1)
            for n, (dst, f) in enumerate(((atok, ACT.Copy), (toend, ACT.Exp), (dec, ACT.Exp))):
                act.activation(dst[:, :, :].rearrange("p c h -> p (c h)"), AX[:, 1, n * P:(n + 1) * P], f).then_inc(
                    atok_ready, 1)

            def v_square(g, j):
                act.wait_ge(yv_ready, 4 * g + (j + 1))
                act.wait_ge(vacc, 4 * g + (17 + j))
                act.activation(sq[:, j % 2, :], tile(yy, 4 * g + j), ACT.Square).then_inc(vsq_ready, 1)

            def decays(g):
                act.wait_ge(atg_done, g + 1)
                if not isinstance(g, int):
                    act.wait_ge(pair_done, 4 * g)
                else:
                    act.wait_ge(pad_zero, 6)
                act.activation(atg[0:8, :], AX[0:8, 1, :], ACT.Copy).then_inc(atg_ready, 1)

            def ssd_group(g):
                later = not isinstance(g, int)
                for j in range(4):
                    hi(g, 8, U_SSD + 2 * j + LEAD)
                    act.wait_ge(unit_used, 8 * g + (U_SSD + 2 * j + 1))
                    act.activation(xr[:, j % 2, 3:], PR[:, (2 * j) % 4, :], ACT.Copy).then_inc(xr_ready, 1)
                    if j == 0 and later:
                        decays(g)
                    act.wait_ge(conv_ready, 4 * g + (9 + j))
                    act.activation(th[:, :], cx[:, j % 2, :], ACT.Tanh, scale=0.5).then_inc(th_ready, 1)
                    if j == 1 and later:
                        rms(g + 5, ss_ready, g + 2, width=4 * 512, bank=1)
                    hi(g, 8, U_SSD + 2 * j + 1 + LEAD)
                    if j > 0 or later:
                        v_square(g, j - 1)
                    act.wait_ge(unit_used, 8 * g + (U_SSD + 2 * j + 2))
                    act.activation(gz[:, :], PR[:, (2 * j + 1) % 4, :], ACT.Tanh, scale=0.5).then_inc(thz_ready, 1)
                    if j == 0 and not later:
                        decays(g)
                    if j == 0:
                        act.wait_ge(btr_done, g + 1)
                        act.activation(btok[:, :, :].rearrange("p a b -> p (a b)"), AX[:, 3, :], ACT.Copy).then_inc(
                            btok_ready, 1)
                    for e in range(2):
                        act.wait_ge(seg_ready, 8 * g + (2 * j + e + 1))
                        act.activation(seg[:, e, :, :], seg[:, e, :, :], ACT.Exp).then_inc(ex_ready, 1)
                    act.wait_ge(pair_done, 4 * g + (j + 1))
                    act.activation(eab[:, :], AX[:, 0, :], ACT.Exp).then_inc(eab_ready, 1)

            ssd_group(0)
            with act.Fori(1, GROUPS) as g:
                ssd_group(g)
            v_square(GROUPS, -1)
            rms(GROUPS + 5, ss_ready, GROUPS + 2, width=4 * 512, bank=1)

            for k in range(16):
                act.wait_ge(yy_ready, 16)
                act.activation(yh[:, k, :], yy[:, k, :], ACT.Copy).then_inc(yh_ready, 1)
            with act.Fori(0, 2) as i:
                for m in range(4):
                    for q in range(3):
                        hi(i, 12, U_MRG + 3 * m + q + LEAD)
                        if q == 0:
                            act.wait_ge(unit_used, 12 * i + (U_MRG + 3 * m + 1))
                            act.activation(sga[:, m % 2, :], PR[:, (2 * m) % 4, :], ACT.Sigmoid).then_inc(sga_ready, 1)
                    act.wait_ge(mrg_ready, 4 * i + (R0 + 9 + m))
                    act.activation(tile(mh, 4 * i + m), tile(mrg, 4 * i + m), ACT.Copy).then_inc(mh_ready, 1)
            with act.Fori(0, 2) as i:
                for j in range(4):
                    hi(i, 4, U_WO + j + LEAD)
            squares(24, 16)
            rms(10, sq_used, 32)
            split_h(24, ht4, h4h)
            feed_forward(2, U_GU2, sg2, ff2, fh2)
            with act.Fori(0, KT - 1) as i:
                for j in range(4):
                    hi(i, 4, U_DN2 + j + LEAD)
            hi(0, 4, U_END - 1)
            squares(32, 24)
            rms(11, sq_used, 40)

        @block.vector
        def _(dve):
            counts = {"upd": 0, "hs": 0, "pool": 0}

            def cols(name, k=0, n=KT):
                return vec[:, V[name] + k:V[name] + k + n]

            def make_h(n_r, first, scale, shift, ht, hh, hl):
                dve.wait_ge(r_ready, n_r)

                def full(k):
                    if first + k >= 2:
                        dve.wait_ge(hl_ready, first + k - 1)
                    ins = dve.scalar_tensor_tensor(ht[:, k % 2, :], x[:, k, :], scale(k), rr[:, :], ALU.mult, ALU.mult)
                    if shift is not None:
                        ins.then_inc(hs_ready, 1)
                        counts["hs"] += 1
                        dve.wait_ge(hs_ready, counts["hs"])
                        ins = dve.tensor_scalar(ht[:, k % 2, :], ht[:, k % 2, :], shift(k), None, ALU.add)
                    ins.then_inc(ht_ready, 1)

                full(0)
                for k in range(KT):
                    if k + 1 < KT:
                        full(k + 1)
                    dve.wait_ge(hh_ready, first + k + 1)
                    dve.wait_ge(ht_ready, first + k + 1)
                    dve.tensor_tensor(hl[:, k, :], ht[:, k % 2, :], hh[:, k, :], ALU.subtract).then_inc(hl_ready, 1)

            def mod_unit(n):
                m, k = n // KT, n % KT
                dve.wait_ge(cond_in[n % RING], 16 * (n // RING + 1))
                if k == 0:
                    if m >= 2:
                        dve.wait_ge(msum_done, m - 1)
                    ins = dve.tensor_scalar(macc[:, m % 2, :], cond[:, n % RING, :], cvec[:, k:k + 1], None, ALU.mult)
                else:
                    dve.wait_ge(cond_used, n)
                    ins = dve.scalar_tensor_tensor(macc[:, m % 2, :], cond[:, n % RING, :], cvec[:, k:k + 1],
                                                   macc[:, m % 2, :], ALU.mult, ALU.add)
                ins.then_inc(cond_used, 1)

            for s in (ff_ready, pr_ready, cv_ready, mrg_ready, sz_ready, ta_ready):
                dve.sem_inc(s, R0)

            for m in (padA, padB, padC):
                dve.memset(m[:, 0:16], 0.0).then_inc(pad_zero, 1)
            dve.wait_ge(cvec_ready, 1)
            for n in range(16):
                mod_unit(n)
            dve.wait_ge(msum_done, 2)
            dve.tensor_tensor(mod[:, 0:16], PR[:, 3, 0:16], cols("b_cond", 0, 16), ALU.add).then_inc(mod_ready, 1)
            dve.wait_ge(mod_ready, 1)
            dve.scalar_tensor_tensor(amix[:, :], mod[:, 8:16], 1.0, cols("g_mix_pre"), ALU.add, ALU.mult).then_inc(
                mod_ready, 1)
            dve.wait_ge(mod_ready, 2)
            dve.wait_ge(s_x, 16)
            make_h(1, 0, lambda k: amix[:, k:k + 1], lambda k: mod[:, k:k + 1], ht1, h1h, h1l)

            def soft_plus(h):
                for n, (c, w, _) in enumerate(PARTS):
                    dve.wait_ge(l_ready, 2 * h + n + 1)
                    if h >= 1:
                        dve.wait_ge(cum_done, 2 * h)
                    dve.scalar_tensor_tensor(sp_[:, c:c + w], AXf[:, c:c + w], 0.0, az[:, c:c + w], ALU.max,
                                             ALU.add).then_inc(sp_ready, 1)

            def pool_step(ins):
                counts["pool"] += 1
                ins.then_inc(pstep, 1)

            def pooling(g):
                dve.wait_ge(qkvu_ready, 4 * g + 4)
                src = padA
                for s in range(g + 1):
                    dst, w = (padB, padC)[s % 2], 1 << s
                    pool_step(dve.tensor_tensor(dst[:, 16:], src[:, 16:], src[:, 16 - w:16 - w + T], ALU.add))
                    dve.wait_ge(pstep, counts["pool"])
                    src = dst
                if g >= 1:
                    dve.wait_ge(pooly_done, g)
                pool_step(dve.scalar_tensor_tensor(pooled[:, :], src[:, 16:], 1.0 / (2 << g), padA[:, 16:], ALU.mult,
                                                   ALU.subtract))
                pool_step(dve.tensor_tensor(pfix[:, :], src[:, 16:32], con_("inv", 16 * g, 16), ALU.mult))
                dve.wait_ge(pstep, counts["pool"])
                dve.tensor_tensor(pooled[:, 0:16], pfix[:, :], padA[:, 16:32], ALU.subtract).then_inc(pooled_ready, 1)

            def pool_low(g):
                dve.wait_ge(poolh_ready, g + 1)
                dve.scalar_tensor_tensor(mixl[:, 4 + g, :], PR[:, 2, :], vec_("pool_scale", g), mixh[:, 4 + g, :],
                                         ALU.mult, ALU.subtract).then_inc(pooll_ready, 1)

            for h in range(HEADS):
                p, e = h // 2, h % 2
                for n in range(16 + 4 * h, 18 + 4 * h):
                    mod_unit(n)
                soft_plus(h)
                for n in range(18 + 4 * h, 20 + 4 * h):
                    mod_unit(n)
                if e == 0:
                    pooling(p)
                if e == 0:
                    pool_low(p)
                else:
                    dve.wait_ge(mixh_ready, p + 1)
                    dve.tensor_tensor(mixl[:, p, :], AX[:, 3, :], mixh[:, p, :], ALU.subtract).then_inc(mixl_ready, 1)

            dve.wait_ge(msum_done, 6)
            dve.tensor_tensor(mod[:, 16:48], PR[:, 3, 16:48], cols("b_cond", 16, 32), ALU.add).then_inc(mod_ready, 1)

            def accumulate(i, per, c, slot):
                dve.wait_ge(msq_ready, per * i + (c + 1))
                dve.wait_ge(vacc, per * i + (c + 1 + c // 8))
                dve.tensor_tensor(ssum[:, :], ssum[:, :], sq[:, slot, :], ALU.add).then_inc(vacc, 1)

            def post_norm(n_r, mix, gate):
                dve.wait_ge(r_ready, n_r)
                for k in range(KT):
                    dve.scalar_tensor_tensor(mix[:, k, :], mix[:, k, :], gate[:, k:k + 1], rr[:, :], ALU.mult,
                                             ALU.mult).then_inc(upd_ready, 1)
                    counts["upd"] += 1
                    if k > 0:
                        dve.wait_ge(upd_ready, counts["upd"] - 1)
                        dve.tensor_tensor(x[:, k - 1, :], x[:, k - 1, :], mix[:, k - 1, :], ALU.add).then_inc(res_ready, 1)
                dve.wait_ge(upd_ready, counts["upd"])
                dve.tensor_tensor(x[:, KT - 1, :], x[:, KT - 1, :], mix[:, KT - 1, :], ALU.add).then_inc(res_ready, 1)

            dve.memset(ssum[:, :], 0.0).then_inc(vacc, 1)
            with dve.Fori(0, 2) as i:
                for j in range(4):
                    accumulate(i, 4, j, j % 2)
            dve.wait_ge(mod_ready, 3)
            dve.tensor_tensor(gmix[:, :], mod[:, 16:24], cols("g_mix_post"), ALU.mult).then_inc(mod_ready, 1)
            dve.scalar_tensor_tensor(affn[:, :], mod[:, 32:40], 1.0, cols("g_ffn_pre"), ALU.add, ALU.mult).then_inc(
                mod_ready, 1)
            dve.tensor_tensor(gffn[:, :], mod[:, 40:48], cols("g_ffn_post"), ALU.mult).then_inc(mod_ready, 1)
            dve.wait_ge(mod_ready, 6)
            post_norm(2, mix1, gmix)
            make_h(3, 8, lambda k: affn[:, k:k + 1], lambda k: mod[:, 24 + k:25 + k], ht2, h2h, h2l)

            def feed_forward(n, first_u, sg, ff, fh, fl):
                done = FT * (n - 1)
                with dve.Fori(0, FT // 2) as i:
                    for b in range(2):
                        dve.wait_ge(sg_ready, 2 * i + (R0 + done + b + 1))
                        dve.wait_ge(unit_used, 4 * i + (first_u + 2 * b + 2))
                        dve.tensor_tensor(ff[:, b, :], sg[:, b, :], PR[:, 2 * b + 1, :], ALU.mult).then_inc(ff_ready, 1)
                        dve.wait_ge(fh_ready, 2 * i + (done + b + 1))
                        dve.tensor_tensor(tile(fl, 2 * i + b), ff[:, b, :], tile(fh, 2 * i + b), ALU.subtract).then_inc(
                            fl_ready, 1)

            feed_forward(1, U_GU1, sg1, ff1, fh1, fl1)
            dve.memset(ssum[:, :], 0.0).then_inc(vacc, 1)
            with dve.Fori(0, KT // 2) as i:
                for b in range(2):
                    accumulate(i, 2, 8 + b, b)
            post_norm(4, mix2, gffn)
            make_h(5, 16, lambda k: cols("norm_mix_w_2", k, 1), None, ht3, h3h, h3l)

            dve.memset(pr[:, :, 0:2], 0.0).then_inc(pad_zero, 1)
            dve.wait_ge(dt_a, 1)
            dve.tensor_tensor(wdtl[:, :, :], wdtr[:, :, :], wdth[:, :, :], ALU.subtract).then_inc(dt_v, 1)
            with dve.Fori(0, 2) as i:
                for m in range(4):
                    dve.wait_ge(c_ready, 4 * i + (R0 + m + 1))
                    dve.wait_ge(unit_used, 12 * i + (U_SC + 3 * m + 2))
                    if m == 0:
                        dve.wait_ge(pad_zero, 4)
                    q = m % 2
                    dve.tensor_tensor(pr[:, q, 2:], cb[:, q, :], PR[:, (3 * m + 1) % 4, :], ALU.mult).then_inc(pr_ready, 1)
                    dve.wait_ge(pr_ready, 4 * i + (R0 + m + 1))
                    dve.tensor_scalar(cv[:, q, :], pr[:, q, 0:T], vec_("sconv_w", 4 * i + m), None, ALU.mult).then_inc(
                        cstep, 1)
                    for k in (1, 2):
                        dve.wait_ge(cstep, 12 * i + (3 * m + k))
                        dve.scalar_tensor_tensor(cv[:, q, :], pr[:, q, k:k + T], vec_("sconv_w", 4 * i + (m + 8 * k)),
                                                 cv[:, q, :], ALU.mult, ALU.add).then_inc(cstep, 1)
                    dve.wait_ge(cstep, 12 * i + (3 * m + 3))
                    dve.wait_ge(unit_used, 12 * i + (U_SC + 3 * m + 3))
                    dve.tensor_tensor(cv[:, q, :], cv[:, q, :], PR[:, (3 * m + 2) % 4, :], ALU.mult).then_inc(cv_ready, 1)
                    dve.wait_ge(vh_ready, 4 * i + (m + 1))
                    dve.tensor_tensor(tile(vl, 4 * i + m), cv[:, q, :], tile(vh, 4 * i + m), ALU.subtract).then_inc(
                        vl_ready, 1)
            with dve.Fori(0, 4) as i:
                for b in range(2):
                    dve.wait_ge(sgb_ready, 2 * i + (R0 + b + 1))
                    dve.wait_ge(unit_used, 4 * i + (U_SCP + 2 * b + 2))
                    dve.tensor_tensor(tile(mrg, 2 * i + b), sgb[:, b, :], PR[:, 2 * b + 1, :], ALU.mult).then_inc(
                        mrg_ready, 1)

            def conv4(i, per, c, chan, slot):
                dve.wait_ge(xr_ready, per * i + (R0 + c + 1))
                dve.tensor_scalar(cx[:, slot, :], xr[:, slot, 0:T], vec_("conv_w", 4 * i + chan),
                                  vec_("conv_b", 4 * i + chan), ALU.mult, ALU.add).then_inc(tap, 1)
                for k in (1, 2, 3):
                    dve.wait_ge(tap, 3 * per * i + (3 * c + k))
                    dve.scalar_tensor_tensor(cx[:, slot, :], xr[:, slot, k:k + T], vec_("conv_w", 4 * i + (chan + 24 * k)),
                                             cx[:, slot, :], ALU.mult, ALU.add).then_inc(tap if k < 3 else conv_ready, 1)

            dve.wait_ge(dt_done, 1)
            dve.tensor_tensor(dta[:, :, :], AX[:, 0, 0:P].rearrange("p (c h) -> p c h", c=NCH),
                              cols("dt_bias", 0, 32).unsqueeze(1).broadcast_to([P, NCH, 32]), ALU.add).then_inc(dt_v, 1)
            dve.wait_ge(dt_v, 2)
            dve.tensor_scalar(dte[:, :, :], dta[:, :, :], 0.0, None, ALU.max).then_inc(dt_v, 1)
            dve.wait_ge(dt_v, 3)
            dve.scalar_tensor_tensor(dte[:, :, :], dte[:, :, :], -2.0, dta[:, :, :], ALU.mult, ALU.add).then_inc(dt_v, 1)
            dve.wait_ge(dt_a, 4)
            dve.scalar_tensor_tensor(dt[:, :, :], dta[:, :, :], 0.0, dte[:, :, :], ALU.max, ALU.add).then_inc(dt_v, 1)
            dve.wait_ge(dt_v, 5)
            dve.scalar_tensor_tensor(da[:, :, :], dt[:, :, :], -1.0, ea[:, :].unsqueeze(1).broadcast_to([P, NCH, 32]),
                                     ALU.mult, ALU.mult).then_inc(dt_v, 1)
            dve.tensor_scalar(dte[:, :, :], dt[:, :, :], 0.5, None, ALU.mult).then_inc(dt_v, 1)
            dve.tensor_scalar(halves[:, 0:16], cols("ssd_norm_w_2", 0, 16), 0.5, None, ALU.mult).then_inc(dt_v, 1)
            dve.tensor_scalar(halves[:, 16:32], cols("d_skip", 0, 16), 0.5, None, ALU.mult).then_inc(dt_v, 1)
            dve.memset(xr[:, :, 0:3], 0.0).then_inc(pad_zero, 1)
            dve.wait_ge(pad_zero, 5)
            with dve.Fori(0, 2) as i:
                for j in range(4):
                    conv4(i, 4, j, 16 + j, j % 2)

            dve.wait_ge(dt_v, 9)
            dve.wait_ge(atok_ready, 3)
            dve.wait_ge(bc_ready, 8)
            dve.memset(atg[:, :].bitcast(F32), 0.0).then_inc(pad_zero, 1)

            def heads(t, g, j, c0=0, c1=NCH, e0=0, n=2):
                return t[:, c0:c1, bass.ds(8 * g + (2 * j + e0), n)]

            def gate(g, j):
                dve.wait_ge(thz_ready, 4 * g + (j + 1))
                dve.scalar_tensor_tensor(gz[:, :], gz[:, :], 1.0, PR[:, (2 * j + 1) % 4, :], ALU.add, ALU.mult).then_inc(
                    sz_ready, 1)

            def gated(g, j):
                dve.wait_ge(y_done, 4 * g + (j + 1))
                dve.scalar_tensor_tensor(yb[:, :], xs[:, j % 2, :], halves[:, bass.ds(4 * g + (16 + j), 1)], AX[:, 2, :],
                                         ALU.mult, ALU.add).then_inc(yb_ready, 1)
                dve.wait_ge(eab_ready, 4 * g + (j + 1))
                dve.tensor_tensor(eab[:, P:], eab[:, P:], AX[:, 3, P:], ALU.mult).then_inc(yo_ready, 1)
                dve.wait_ge(yb_ready, 4 * g + (j + 1))
                dve.wait_ge(yo_ready, 4 * g + (j + 1))
                dve.tensor_tensor(yb[:, P:], yb[:, P:], eab[:, P:], ALU.add).then_inc(y2_ready, 1)
                dve.wait_ge(sz_ready, 4 * g + (R0 + j + 1))
                dve.wait_ge(y2_ready, 4 * g + (j + 1))
                dve.tensor_tensor(tile(yy, 4 * g + j), yb[:, :], gz[:, :], ALU.mult).then_inc(yv_ready, 1)

            def add_square(g, j):
                dve.wait_ge(vsq_ready, 4 * g + (j + 1))
                if j == 0:
                    dve.tensor_copy(ssum[:, :], sq[:, 0, :]).then_inc(vacc, 1)
                else:
                    dve.wait_ge(vacc, 4 * g + (18 + j))
                    dve.tensor_tensor(ssum[:, :], ssum[:, :], sq[:, j % 2, :], ALU.add).then_inc(vacc, 1)

            def norm_group(g):
                dve.wait_ge(r_ready, g + 5)
                for k in range(-4, 0):
                    dve.scalar_tensor_tensor(tile(yy, 4 * g + k), tile(yy, 4 * g + k), halves[:, bass.ds(4 * g + k, 1)],
                                             rr[:, :], ALU.mult, ALU.mult).then_inc(yy_ready, 1)

            def ssd_group(g):
                later = not isinstance(g, int)
                dve.tensor_copy(bt[:, :], tile(bc, g)).then_inc(grp_ready, 1)
                dve.tensor_copy(dag[:, :, :], da[:, :, bass.ds(8 * g, 8)]).then_inc(grp_ready, 1)
                if not later:
                    dve.tensor_copy(ct[:, :], tile(bc, g + 4)).then_inc(grp_ready, 1)
                for j in range(4):
                    conv4(g, 4, 8 + j, j, j % 2)
                    if j > 0 or later:
                        gate(g, j - 1)
                    dve.wait_ge(th_ready, 4 * g + (j + 1))
                    dve.scalar_tensor_tensor(xs[:, j % 2, :], th[:, :], 1.0, cx[:, j % 2, :], ALU.add, ALU.mult).then_inc(
                        xs_ready, 1)
                    if j > 0 or later:
                        gated(g, j - 1)
                    if j == 0 and later:
                        dve.tensor_copy(ct[:, :], tile(bc, g + 4)).then_inc(grp_ready, 1)
                    if j == 0:
                        dve.wait_ge(atg_ready, g + 1)
                        dve.tensor_tensor(atg[32:40, :], AX[0:8, 1, :], atg[0:8, :], ALU.subtract).then_inc(atgl_ready, 1)
                    if j == 0:
                        if later:
                            add_square(g, -1)
                        dve.wait_ge(cb_done, g + 1)
                        dve.tensor_tensor(cbm[:, :, :], AX[:, 2, :].rearrange("p (c l) -> p c l", c=NCH),
                                          con_("upto").unsqueeze(1).broadcast_to([P, NCH, P]), ALU.mult).then_inc(
                                              cbm_ready, 1)
                    dve.wait_ge(xtr_done, 4 * g + (j + 1))
                    dve.tensor_tensor(xdt[:, :, :].rearrange("p c (e d) -> p c e d", e=2),
                                      AX[:, 3, :].rearrange("p (c e d) -> p c e d", c=NCH, e=2),
                                      spread(heads(dte, g, j), [P, NCH, 2, 64]), ALU.mult).then_inc(xdt_ready, 1)
                    dve.wait_ge(xdt_ready, 4 * g + (j + 1))
                    dve.tensor_tensor(xde[:, :, :].rearrange("p c (e d) -> p c e d", e=2),
                                      xdt[:, 0:3, :].rearrange("p c (e d) -> p c e d", e=2),
                                      spread(heads(toend, g, j, 0, 3), [P, 3, 2, 64]), ALU.mult).then_inc(xde_ready, 1)
                    for e in range(2):
                        dve.wait_ge(abc_done, 8 * g + (2 * j + e + 1))
                        for c in range(NCH):
                            ins = dve.tensor_scalar(seg[:, e, c, :], AX[:, e, c * P:(c + 1) * P],
                                                    atok[:, c, bass.ds(8 * g + (2 * j + e), 1)], 0.0, ALU.subtract,
                                                    ALU.min)
                        ins.then_inc(seg_ready, 1)
                    dve.wait_ge(stp_done, 4 * g + (j + 1))
                    dve.tensor_copy(st[:, 0, :], AX[:, 3, 0:P]).then_inc(st_step, 1)
                    for c in (1, 2):
                        dve.wait_ge(st_step, 20 * g + (5 * j + 2 * c - 1))
                        dve.tensor_tensor(st[:, c, :].rearrange("p (e d) -> p e d", e=2),
                                          st[:, c - 1, :].rearrange("p (e d) -> p e d", e=2),
                                          spread(heads(dec, g, j, c, c + 1).rearrange("p c e -> p (c e)"), [P, 2, 64]),
                                          ALU.mult).then_inc(st_step, 1)
                        dve.wait_ge(st_step, 20 * g + (5 * j + 2 * c))
                        dve.tensor_tensor(st[:, c, :], st[:, c, :], AX[:, 3, c * P:(c + 1) * P], ALU.add).then_inc(
                            st_step, 1)
                    for e in range(2):
                        dve.wait_ge(ex_ready, 8 * g + (2 * j + e + 1))
                        dve.tensor_tensor(seg[:, e, :, :], seg[:, e, :, :], cbm[:, :, :], ALU.mult).then_inc(sc_ready, 1)
                    if j == 1 and later:
                        norm_group(g)
                    if j > 0:
                        add_square(g, j - 1)

            ssd_group(0)
            with dve.Fori(1, GROUPS) as g:
                ssd_group(g)
            gate(GROUPS, -1)
            gated(GROUPS, -1)
            add_square(GROUPS, -1)
            norm_group(GROUPS)

            for k in range(16):
                dve.wait_ge(yh_ready, k + 1)
                dve.tensor_tensor(yl[:, k, :], yy[:, k, :], yh[:, k, :], ALU.subtract).then_inc(yl_ready, 1)
            with dve.Fori(0, 2) as i:
                for m in range(4):
                    dve.wait_ge(sga_ready, 4 * i + (R0 + m + 1))
                    dve.wait_ge(unit_used, 12 * i + (U_MRG + 3 * m + 3))
                    dve.tensor_tensor(ta[:, m % 2, :], sga[:, m % 2, :], PR[:, (2 * m + 1) % 4, :], ALU.mult).then_inc(
                        ta_ready, 1)
                    dve.wait_ge(ta_ready, 4 * i + (R0 + m + 1))
                    dve.tensor_tensor(tile(mrg, 4 * i + m), tile(mrg, 4 * i + m), ta[:, m % 2, :], ALU.add).then_inc(
                        mrg_ready, 1)
                    dve.wait_ge(mh_ready, 4 * i + (m + 1))
                    dve.tensor_tensor(tile(ml, 4 * i + m), tile(mrg, 4 * i + m), tile(mh, 4 * i + m),
                                      ALU.subtract).then_inc(ml_ready, 1)
            with dve.Fori(0, 2) as i:
                for j in range(4):
                    dve.wait_ge(unit_used, 4 * i + (U_WO + j + 1))
                    dve.tensor_tensor(tile(x, 4 * i + j), tile(x, 4 * i + j), PR[:, j, :], ALU.add).then_inc(res_ready, 1)
            make_h(10, 24, lambda k: cols("norm_ffn_w_2", k, 1), None, ht4, h4h, h4l)
            feed_forward(2, U_GU2, sg2, ff2, fh2, fl2)
            with dve.Fori(0, KT // 2) as i:
                for b in range(2):
                    dve.wait_ge(unit_used, 8 * i + (U_DN2 + 4 * b + 4))
                    dve.tensor_tensor(tile(x, 2 * i + b), tile(x, 2 * i + b), PR[:, b, :], ALU.add).then_inc(res_ready, 1)
            dve.wait_ge(r_ready, 11)
            for k in range(KT):
                dve.scalar_tensor_tensor(outT[:, k, :], x[:, k, :], cols("final_norm_w_2", k, 1), rr[:, :], ALU.mult,
                                         ALU.mult).then_inc(out_ready, 1)


def kernel(**inputs):
    import numpy as np
    import concourse.bacc as bacc
    from concourse.bass_utils import run_bass_kernel_spmd

    a = {k: np.asarray(v) for k, v in inputs.items()}

    def tiles(w):
        k, n = w.shape
        return w.reshape(k // P, P, n // P, P).transpose(2, 1, 0, 3).reshape(n // P, P, k)

    def paired(*ws):
        return [b for bs in zip(*ws) for b in bs]

    w_in, w2 = tiles(a["w_in"][0]), a["w_in_2"][0]
    z, xs, b_, c_ = (tiles(w2[:, s:s + n]) for s, n in ((0, 2048), (2048, 2048), (4096, 512), (4608, 512)))
    s_b, s_c, s_x, g_a, g_b = (tiles(w2[:, s:s + 1024]) for s in range(5152, 10272, 1024))
    ssd = tiles(a["w_ssd_proj_2"][0]).reshape(8, P, 2, 1024)
    w8 = np.stack(
        [w_in[4 * kind + p] for p in range(4) for kind in range(4)]
        + list(tiles(a["w_out"][0]))
        + paired(tiles(a["w_gate"][0]), tiles(a["w_up"][0]))
        + paired(s_c, s_x, s_b)
        + paired(g_b, tiles(a["w_sconv_proj_2"][0]))
        + list(b_) + list(c_)
        + paired(xs, z)
        + paired(g_a, ssd[:, :, 0], ssd[:, :, 1])
        + list(tiles(a["w_o_2"][0]))
        + paired(tiles(a["w_gate_2"][0]), tiles(a["w_up_2"][0])))
    w22 = np.concatenate([tiles(a["w_down"][0]), tiles(a["w_down_2"][0])])
    wcond = a["w_cond"][0].reshape(KT, P, 6, D).transpose(2, 0, 1, 3).reshape(6 * KT, P, D)
    wdt = np.ascontiguousarray(w2[:, 5120:5152].reshape(KT, P, 32).transpose(1, 0, 2))
    wpool = np.ascontiguousarray(a["w_pool"][0].transpose(1, 0, 2))

    def column(v):
        return np.asarray(v).reshape(-1, P).T

    cols = [column(a["c"]), column(a["b_cond"]), column(a["g_mix_pre"]), column(a["g_mix_post"]), column(a["g_ffn_pre"]),
            column(a["g_ffn_post"]), column(a["pool_scale"]), column(a["norm_mix_w_2"]), column(a["ssd_conv_w_2"]),
            column(a["ssd_conv_b_2"]), column(a["ssd_norm_w_2"]), column(a["sconv_w_2"]), column(a["norm_ffn_w_2"]),
            column(a["final_norm_w_2"]), column(np.repeat(a["d_skip_2"][0], 64)),
            np.repeat(a["dt_bias_2"], P, axis=0), np.repeat(a["a_log_2"], P, axis=0),
            np.full((P, 1), EPS, np.float32)]
    vecs = np.ascontiguousarray(np.concatenate(cols, axis=1))
    assert vecs.shape == (P, NV)

    i, j = np.arange(P)[:, None], np.arange(P)[None, :]
    inv = np.concatenate([1.0 / np.minimum(np.arange(1, 17), 2 << g) for g in range(4)])[None, :].repeat(P, 0)
    atts = np.stack([i == j, np.where(i >= j, -2.0 ** 100, 0.0), -1.0 * (i >= j), -np.ones((P, P))], axis=1).astype(np.float32)
    q, row = np.arange(8 * P)[None, :], np.arange(40)[:, None]
    row = np.where((row < 8) | (row >= 32), row % 32, -1)
    sels = np.concatenate([row == q // P, row == (q[:, :4 * P] // P) * 2 + (q[:, :4 * P] % P) // 64],
                          axis=1).astype(np.float32)
    cons = np.concatenate([np.ones((P, P)), i > j, i <= j, i == j, inv], axis=1).astype(np.float32)
    assert cons.shape == (P, NC)

    xin = np.ascontiguousarray(a["x"][0].reshape(T, KT, P).transpose(2, 1, 0))
    arrays = dict(w8=w8, w22=w22, wcond=wcond, wdt=wdt, wpool=wpool, vecs=vecs, cons=cons, atts=atts, sels=sels, xin=xin)
    arrays = {n: np.ascontiguousarray(v) for n, v in arrays.items()}
    nc = bacc.Bacc("TRN2", target_bir_lowering=False, num_devices=1, dynamic_dma_scratch_size=1024)
    args = [nc.dram_tensor(n, v.shape, F32, kind="ExternalInput").ap() for n, v in arrays.items()]
    out = nc.dram_tensor("out", (P, KT, T), F32, kind="ExternalOutput").ap()
    hybrid_blocks(nc, *args, out)
    r = run_bass_kernel_spmd(nc, [arrays], core_ids=[0])
    return np.ascontiguousarray(r.results[0]["out"].transpose(2, 1, 0).reshape(1, T, D))
```

```python
from contextlib import ExitStack

import concourse.bass as bass
from concourse import mybir

F32 = mybir.dt.float32
F32R = mybir.dt.float32r
ALU = mybir.AluOpType
ACT = mybir.ActivationFunctionType

P = 128
T = 512
D = 1024
KT = D // P
FT = 2816 // P
NCH = T // P
EPS = 1e-6
RING = 4
R0 = 4
LEAD = 3

HEADS = 8
KEYS = [(0, 0), (1, 512), (3, 896), (2, 1024)]
KCOL = dict(KEYS)
NZ = 1280
PARTS = [(T, NZ - T, [(1, 512), (3, 896), (2, 1024)]), (0, T, [(0, 0)])]

GROUPS = 4
BY_POOL = (1, 3)
DOWN_K = [(0, 6), (6, 6), (12, 5), (17, 5)]

U_IN, U_OUT, U_GU1, U_DN1 = 0, 16, 24, 68
U_SC, U_SCP, U_BC, U_SSD, U_MRG, U_WO = 100, 124, 140, 148, 180, 204
U_GU2, U_DN2, U_END = 212, 256, 288

HL_WO = 3 * (KT - len(BY_POOL))
RES_WO = 2 * (KT - len(BY_POOL))
V_OUT, V_DN1, V_SSD, V_WO, V_DN2 = 1, 10, 18, 35, 44

_VECS = [("c", 8), ("b_cond", 48), ("g_mix_pre", 8), ("g_mix_post", 8), ("g_ffn_pre", 8), ("g_ffn_post", 8),
         ("pool_scale", 4), ("norm_mix_w_2", 8), ("conv_w", 96), ("conv_b", 24), ("ssd_norm_w_2", 16),
         ("sconv_w", 24), ("norm_ffn_w_2", 8), ("final_norm_w_2", 8), ("d_skip", 16), ("dt_bias", 32),
         ("a_log", 32), ("eps", 1)]
V, NV = {}, 0
for _n, _k in _VECS:
    V[_n] = NV
    NV += _k

_CONS = [("ones", 128), ("after", 128), ("upto", 128), ("ident", 128), ("inv", 64)]
NSEL = 12 * P
C, NC = {}, 0
for _n, _k in _CONS:
    C[_n] = NC
    NC += _k


def hybrid_blocks(nc, w8, w22, wcond, wdt, wpool, vecs, cons, atts, sels, xin, out):
    ctx = ExitStack()

    def sb(name, shape, dt=F32, stack=ctx):
        return stack.enter_context(nc.sbuf_tensor(name, shape, dt))

    def sem(name):
        return ctx.enter_context(nc.semaphore(name))

    with ctx:
        con = sb("con", [P, NC])
        with ExitStack() as over:
            sel_raw = sb("sel_raw", [40, NSEL], F32, over)
        sel = sb("sel", [40, NSEL], F32R)
        vec = sb("vec", [P, NV])
        x = sb("x", [P, KT, T])
        raw = sb("raw", [P, RING, 1024])
        whi = sb("whi", [P, RING, 1024], F32R)
        wlo = sb("wlo", [P, RING, 1024], F32R)
        rr = sb("rr", [P, T])
        sq = sb("sq", [P, 2, T])
        ssum = sb("ssum", [P, T])
        cvec = sb("cvec", [P, KT])
        mod = sb("mod", [P, 48])
        amix = sb("amix", [P, KT])
        gmix = sb("gmix", [P, KT])
        affn = sb("affn", [P, KT])
        gffn = sb("gffn", [P, KT])
        halves = sb("halves", [P, 32])
        wdtr = sb("wdtr", [P, KT, 32])

        def region(build):
            with ExitStack() as s:
                return build(lambda name, shape, dt=F32, stack=s: sb(name, shape, dt, stack))

        def phase_a(a):
            t = dict(mixh=a("mixh", [P, KT, T], F32R), mixl=a("mixl", [P, KT, T], F32R),
                     h1h=a("h1h", [P, KT, T], F32R), h1l=a("h1l", [P, KT, T], F32R), cond=a("cond", [P, RING, 1024]),
                     macc=a("macc", [P, 2, 1024]),
                     att=a("att", [P, 4, P]), late=a("late", [P, 4, P], F32R))
            with ExitStack() as s:
                t.update(mix1=a("mix1", [P, KT, T], F32, s))
            with ExitStack() as s:
                t.update(az=a("az", [P, NZ], F32, s), sp_=a("sp", [P, NZ], F32, s))
            t.update(sph=a("sph", [P, NZ], F32R), spl=a("spl", [P, NZ], F32R))
            t.update(qT=a("qT", [P, 2, T]), kT=a("kT", [P, 2, T]), vT=a("vT", [P, T]), vtok=a("vtok", [P, 2, NCH, P]),
                     pw=a("pw", [P, NZ]),
                     padA=a("padA", [P, 16 + T]), padB=a("padB", [P, 16 + T]), padC=a("padC", [P, 16 + T]),
                     pooled=a("pooled", [P, T]), wp=a("wp", [P, 4, P]), ht1=a("ht1", [P, RING, T]),
                     pfix=a("pfix", [P, 16]))
            return t.values()
        (mixh, mixl, h1h, h1l, cond, macc, att, late, mix1, az, sp_, sph, spl, qT, kT, vT, vtok, pw, padA, padB, padC, pooled, wp,
         ht1, pfix) = region(phase_a)

        def phase_f(n):
            def build(a):
                fh, fl = a(f"fh{n}", [P, FT, T], F32R), a(f"fl{n}", [P, FT, T], F32R)
                with ExitStack() as s:
                    mix = a(f"mixf{n}", [P, KT, T], F32, s)
                return (fh, fl, mix, a(f"hf{n}h", [P, KT, T], F32R), a(f"hf{n}l", [P, KT, T], F32R),
                        a(f"htf{n}", [P, RING, T]), a(f"sg{n}", [P, 2, T]), a(f"ff{n}", [P, 2, T]))
            return build
        fh1, fl1, mix2, h2h, h2l, ht2, sg1, ff1 = region(phase_f(1))
        fh2, fl2, outT, h4h, h4l, ht4, sg2, ff2 = region(phase_f(2))

        def phase_e(a):
            t = dict(h3h=a("h3h", [P, KT, T], F32R), h3l=a("h3l", [P, KT, T], F32R))
            with ExitStack() as s:
                t.update(ml=a("ml", [P, KT, T], F32R, s))
            t.update(mrg=a("mrg", [P, KT, T]))
            with ExitStack() as s:
                t.update(vh=a("vh", [P, KT, T], F32R, s), vl=a("vl", [P, KT, T], F32R, s))
                with ExitStack() as s2:
                    t.update(ht3=a("ht3", [P, RING, T], F32, s2))
                a("below_cb", [P, 2, T], F32, s)
                t.update(
                         cb=a("cb", [P, 2, T], F32, s), pr=a("pr", [P, 2, 2 + T], F32, s), cv=a("cv", [P, 2, T], F32, s),
                         sgb=a("sgb", [P, 2, T], F32, s))
            with ExitStack() as s:
                t.update(mh=a("mh", [P, KT, T], F32R, s))
            t.update(bc=a("bc", [P, 8, T]))
            with ExitStack() as s:
                a("beside_vl", [P, KT, T], F32, s)
                t.update(wdth=a("wdth", [P, KT, 32], F32R, s),
                         wdtl=a("wdtl", [P, KT, 32], F32R, s))
            with ExitStack() as s:
                t.update(yl=a("yl", [P, 16, T], F32R, s), yh=a("yh", [P, 16, T], F32R, s),
                         sga=a("sga", [P, 2, T], F32, s), ta=a("ta", [P, 2, T], F32, s))
            t.update(yy=a("yy", [P, 16, T]))
            t.update(bt=a("bt", [P, T]), ct=a("ct", [P, T]), dag=a("dag", [P, NCH, 8]))
            t.update(dt=a("dt", [P, NCH, 32]), dte=a("dte", [P, NCH, 32]), da=a("da", [P, NCH, 32]),
                     dta=a("dta", [P, NCH, 32]), ea=a("ea", [P, 32]),
                     atok=a("atok", [P, NCH, 32]), toend=a("toend", [P, NCH, 32]), dec=a("dec", [P, NCH, 32]),
                     cbm=a("cbm", [P, NCH, P]),
                     btok=a("btok", [P, NCH, P]), atg=a("atg", [40, T], F32R),
                     xr=a("xr", [P, 2, 3 + T]), cx=a("cx", [P, 2, T]), th=a("th", [P, T]), xs=a("xs", [P, 2, T]),
                     xdt=a("xdt", [P, NCH, P]), xde=a("xde", [P, 3, P]), seg=a("seg", [P, 2, NCH, P]),
                     st=a("st", [P, 3, P]), eab=a("eab", [P, T]), yb=a("yb", [P, T]), gz=a("gz", [P, T]))
            return t.values()
        (h3h, h3l, ml, mrg, vh, vl, ht3, cb, pr, cv, sgb, mh, bc, wdth, wdtl, yl, yh, sga, ta, yy, bt, ct, dag, dt, dte, da,
         dta, ea, atok, toend, dec, cbm, btok, atg, xr, cx, th, xs, xdt, xde, seg, st, eab, yb,
         gz) = region(phase_e)

        PR = ctx.enter_context(nc.psum_tensor("PR", [P, 4, T], F32))
        AX = ctx.enter_context(nc.psum_tensor("AX", [P, 4, T], F32))
        AXf = AX[:, :, :].rearrange("p a b -> p (a b)")

        raw_in = [sem(f"raw_in{j}") for j in range(RING)]
        cond_in = [sem(f"cond_in{j}") for j in range(RING)]
        s_con, s_x, s_wdt, s_out, out_ready = map(sem, ("s_con", "s_x", "s_wdt", "s_out", "out_ready"))
        hi_ready, lo_ready, unit_used, cond_used = map(sem, ("hi_ready", "lo_ready", "unit_used", "cond_used"))
        cvec_ready, mod_ready, msum_done = map(sem, ("cvec_ready", "mod_ready", "msum_done"))
        sq_ready, sq_used, ss_ready, ln_ready, r_ready = map(sem, ("sq_ready", "sq_used", "ss_ready", "ln_ready", "r_ready"))
        msq_ready, vacc = map(sem, ("msq_ready", "vacc"))
        ht_ready, hs_ready, hh_ready, hl_ready, hl_pool, upd_ready, res_ready, res_pool = map(
            sem, ("ht_ready", "hs_ready", "hh_ready", "hl_ready", "hl_pool", "upd_ready", "res_ready", "res_pool"))
        qkvu_ready, vtr_done, vtok_ready = map(sem, ("qkvu_ready", "vtr_done", "vtok_ready"))
        late_ready, z_done, az_ready, e_ready, l_ready, sp_ready, sph_ready, spl_ready = map(
            sem, ("late_ready", "z_done", "az_ready", "e_ready", "l_ready", "sp_ready", "sph_ready", "spl_ready"))
        cum_done, w_ready, pv_done, mixh_ready, mixl_ready = map(
            sem, ("cum_done", "w_ready", "pv_done", "mixh_ready", "mixl_ready"))
        pad_zero, pstep, pooled_ready, pooly_done, poolh_ready, pooll_ready = map(
            sem, ("pad_zero", "pstep", "pooled_ready", "pooly_done", "poolh_ready", "pooll_ready"))
        gs_ready, us_ready = map(sem, ("gs_ready", "us_ready"))
        mix_ready, sg_ready, ff_ready, fh_ready, fl_ready = map(
            sem, ("mix_ready", "sg_ready", "ff_ready", "fh_ready", "fl_ready"))
        c_ready, pr_ready, cstep, cv_ready, vh_ready, vl_ready, sgb_ready, mrg_ready = map(
            sem, ("c_ready", "pr_ready", "cstep", "cv_ready", "vh_ready", "vl_ready", "sgb_ready", "mrg_ready"))
        xr_ready, tap, conv_ready, bc_ready, dt_done, dt_v, dt_a, acum_done, atok_ready = map(
            sem, ("xr_ready", "tap", "conv_ready", "bc_ready", "dt_done", "dt_v", "dt_a", "acum_done", "atok_ready"))
        grp_ready, cb_done, btr_done, atg_done, cbm_ready, btok_ready, atg_ready, atgl_ready, sel_ready = map(
            sem, ("grp_ready", "cb_done", "btr_done", "atg_done", "cbm_ready", "btok_ready", "atg_ready", "atgl_ready",
                  "sel_ready"))
        th_ready, xs_ready, xtr_done, xdt_ready, xde_ready, abc_done, seg_ready, ex_ready, sc_ready = map(
            sem, ("th_ready", "xs_ready", "xtr_done", "xdt_ready", "xde_ready", "abc_done", "seg_ready", "ex_ready",
                  "sc_ready"))
        pair_done, eab_ready, stp_done, st_step, y_done, yb_ready, yo_ready, y2_ready = map(
            sem, ("pair_done", "eab_ready", "stp_done", "st_step", "y_done", "yb_ready", "yo_ready", "y2_ready"))
        thz_ready, sz_ready, yv_ready, vsq_ready, yy_ready = map(
            sem, ("thz_ready", "sz_ready", "yv_ready", "vsq_ready", "yy_ready"))
        yh_ready, yl_ready, sga_ready, ta_ready, mh_ready, ml_ready = map(
            sem, ("yh_ready", "yl_ready", "sga_ready", "ta_ready", "mh_ready", "ml_ready"))

        block = ctx.enter_context(nc.Block())

        def con_(name, lo=0, n=P, rows=P):
            return con[0:rows, C[name] + lo:C[name] + lo + n]

        def vec_(name, k):
            return vec[:, bass.ds(k + V[name], 1)]

        def tile(t, k):
            return t[:, bass.ds(k, 1), :].rearrange("p a b -> p (a b)")

        def shared(by_vector, by_pool, n, k):
            if k in BY_POOL:
                return by_pool, len(BY_POOL) * n + BY_POOL.index(k) + 1
            return by_vector, (KT - len(BY_POOL)) * n + k + 1 - sum(b < k for b in BY_POOL)

        def lo_part(n, k):
            return shared(hl_ready, hl_pool, n, k)

        def spread(ap, shape):
            return ap.unsqueeze(len(ap.shape)).broadcast_to(shape)

        @block.sync
        def _(sp):
            def load_unit(u, j, src):
                if not isinstance(u, int) or u >= RING:
                    sp.wait_ge(lo_ready, u - (RING - 1))
                sp.dma_start(raw[:, j, 0:src.shape[-1]], src).then_inc(raw_in[j], 16)

            def load_cond(n, j):
                if not isinstance(n, int) or n >= RING:
                    sp.wait_ge(cond_used, n - (RING - 1))
                sp.dma_start(cond[:, j, :], wcond[bass.ds(n, 1), :, :].rearrange("a p n -> (a p) n")).then_inc(
                    cond_in[j], 16)

            def w8_at(u):
                return w8[bass.ds(u, 1), :, :].rearrange("a p n -> (a p) n")

            def stream(first, end, at=0):
                with sp.Fori(0, (end - first) // RING) as i:
                    for j in range(RING):
                        load_unit(RING * i + (first + j), j, w8_at(RING * i + (first + j - at)))

            def down(first, block0):
                with sp.Fori(0, KT) as i:
                    for j, (k0, n) in enumerate(DOWN_K):
                        load_unit(RING * i + (first + j), j,
                                  w22[bass.ds(i + block0, 1), :, k0 * P:(k0 + n) * P].rearrange("a p n -> (a p) n"))

            sp.dma_start(vec[:, :], vecs[:, :]).then_inc(s_con, 16)
            sp.dma_start(x[:, :, :], xin[:, :, :]).then_inc(s_x, 16)
            sp.dma_start(con[:, :], cons[:, :]).then_inc(s_con, 16)
            sp.dma_start(att[:, :, :], atts[:, :, :]).then_inc(s_con, 16)
            for n in range(RING):
                load_cond(n, n)
            with sp.Fori(0, 2) as i:
                for j in range(RING):
                    load_cond(RING * i + (RING + j), j)
            load_unit(0, 0, w8_at(0))
            for n in range(12, 16):
                load_cond(n, n % RING)
            for u in range(1, RING):
                load_unit(u, u, w8_at(u))
            sp.dma_start(wp[:, :, :], wpool[:, :, :]).then_inc(s_con, 16)
            sp.dma_start(sel_raw[:, :], sels[:, :]).then_inc(s_con, 16)
            sp.dma_start(wdtr[:, :, :], wdt[:, :, :]).then_inc(s_wdt, 16)
            for j in range(RING):
                load_unit(RING + j, j, w8_at(RING + j))
            for j in range(RING):
                load_cond(16 + j, j)

            def for_head(i, e):
                for j in (2 * e, 2 * e + 1):
                    load_unit(4 * i + (8 + j), j, w8_at(4 * i + (8 + j)))
                for j in range(RING):
                    load_cond(8 * i + (20 + 4 * e + j), j)

            with sp.Fori(0, 3) as i:
                for_head(i, 0)
                for_head(i, 1)
            for_head(3, 0)
            for u in (22, 23):
                load_unit(u, u % RING, w8_at(u))
            stream(U_GU1, U_DN1)
            down(U_DN1, 0)
            stream(U_SC, U_DN2, 32)
            down(U_DN2, KT)
            for k in range(KT):
                sp.wait_ge(out_ready, k + 1)
                sp.dma_start(out[:, k, :], outT[:, k, :]).then_inc(s_out, 16)
            sp.wait_ge(s_out, 16 * KT)

        @block.gpsimd
        def _(pool):
            def lo(i, c):
                j = c % RING
                pool.wait_ge(hi_ready, RING * i + (c + 1))
                pool.tensor_tensor(wlo[:, j, :], raw[:, j, :], whi[:, j, :], ALU.subtract).then_inc(lo_ready, 1)

            def units(first, end):
                with pool.Fori(0, (end - first) // RING) as i:
                    for j in range(RING):
                        lo(i, first + j)

            def residual(n, mix):
                for k in BY_POOL:
                    pool.wait_ge(upd_ready, KT * n + k + 1)
                    pool.tensor_tensor(x[:, k, :], x[:, k, :], mix[:, k, :], ALU.add).then_inc(res_pool, 1)

            def lo_parts(n, ht, hh, hl):
                for k in BY_POOL:
                    pool.wait_ge(hh_ready, KT * n + k + 1)
                    pool.tensor_tensor(hl[:, k, :], ht[:, k % RING, :], hh[:, k, :], ALU.subtract).then_inc(hl_pool, 1)

            for u in range(LEAD):
                lo(0, u)
            lo_parts(0, ht1, h1h, h1l)
            units(LEAD, U_GU1 + LEAD)
            residual(0, mix1)
            lo_parts(1, ht2, h2h, h2l)
            units(U_GU1 + LEAD, U_SC + LEAD)
            residual(1, mix2)
            lo_parts(2, ht3, h3h, h3l)
            units(U_SC + LEAD, U_END - 1)
            lo(0, U_END - 1)

        @block.tensor
        def _(pe):
            def banks(taken, nb=4):
                n = len(taken)

                def wait(i, j):
                    it, pos = (i, j - nb) if j >= nb else (i - 1, j - nb + n)
                    s, base = taken[pos]
                    each = sum(r[0] is s for r in taken)
                    upto = sum(r[0] is s for r in taken[:pos + 1])
                    if j >= nb:
                        pe.wait_ge(s, i * each + (base + upto))
                    else:
                        pe.wait_ge(s, i * each + (base + upto - each))
                return wait

            def unit(u, j, oh, ol, k0, n, bank, first=True, last=True, each=None, halfway=None):
                pe.wait_ge(lo_ready, u + 1)
                for k in range(n):
                    if each is not None:
                        pe.wait_ge(*each(k))
                    if k == n // 2 and halfway is not None:
                        halfway()
                    w = slice(k * P, (k + 1) * P)
                    pe.matmul(bank, whi[:, j, w], oh[:, k0 + k, :], start=first and k == 0, stop=False)
                    pe.matmul(bank, whi[:, j, w], ol[:, k0 + k, :], start=False, stop=False)
                    mm = pe.matmul(bank, wlo[:, j, w], oh[:, k0 + k, :], start=False, stop=last and k == n - 1)
                mm.then_inc(unit_used, 1)

            def sumsq(first):
                for k in range(KT):
                    pe.wait_ge(sq_ready, first + k + 1)
                    mm = pe.matmul(AX[:, 0, :], con_("ones"), sq[:, k % 2, :], start=k == 0, stop=k == KT - 1)
                    mm.then_inc(sq_used, 1)

            def sum_once(n):
                pe.wait_ge(vacc, n)
                pe.matmul(AX[:, 0, :], con_("ones"), ssum[:, :], start=True, stop=True).then_inc(ss_ready, 1)

            def mod_sum(m):
                pe.wait_ge(cond_used, KT * (m + 1))
                if m == 2:
                    pe.wait_ge(mod_ready, 1)
                for k in range(KT):
                    mm = pe.matmul(PR[:, 3, KT * m + k:KT * m + k + 1], macc[:, m % 2, k * P:(k + 1) * P],
                                   con_("ones", 0, 1), start=True, stop=True)
                mm.then_inc(msum_done, 1)

            pe.wait_ge(s_con, 48)
            sumsq(0)
            mod_sum(0)
            mod_sum(1)

            def in_unit(u):
                if u >= 2:
                    pe.wait_ge(qkvu_ready, u - 1)
                unit(u, u % RING, h1h, h1l, 0, KT, PR[:, u % 2, :],
                     each=(lambda k: lo_part(0, k)) if u == 0 else None)

            def v_turn(p):
                pe.wait_ge(qkvu_ready, 4 * p + 3)
                if p >= 1:
                    pe.wait_ge(pooll_ready, p)
                for c in range(NCH):
                    mm = pe.transpose(PR[:, 2, c * P:(c + 1) * P], vT[:, c * P:(c + 1) * P], con_("ident"))
                mm.then_inc(vtr_done, 1)

            def scores(h):
                p, r = h // 2, slice(64 * (h % 2), 64 * (h % 2) + 64)
                pe.wait_ge(qkvu_ready, 4 * p + 2)
                if h == 0:
                    pe.wait_ge(mod_ready, 1)
                    pe.wait_ge(late_ready, 1)
                for n, (_, _, blocks) in enumerate(PARTS):
                    if h >= 1:
                        pe.wait_ge(w_ready, 2 * h - 1 + n)
                    for j, c in blocks:
                        pe.matmul(AXf[:, c:c + T - j * P], kT[r, p % 2, j * P:(j + 1) * P], qT[r, p % 2, j * P:T],
                                  start=j != 3, stop=False, skip_group_check=True)
                    for j, c in blocks:
                        mm = pe.matmul(AXf[:, c:c + P], late[:, 0, :], late[:, 1, :], start=False, stop=False,
                                       skip_group_check=True)
                    mm.then_inc(z_done, 1)

            def later_keys(h):
                for n, (_, _, blocks) in enumerate(PARTS):
                    for part, ready in ((sph, sph_ready), (spl, spl_ready)):
                        pe.wait_ge(ready, 2 * h + n + 1)
                        for j, c in blocks:
                            mm = pe.matmul(AXf[:, c:c + T - j * P], late[:, 2, :], part[:, c:c + T - j * P],
                                           start=False, stop=part is spl and j == NCH - 1, skip_group_check=True)
                            for j2 in range(j + 1, NCH):
                                c2, off = KCOL[j2], c + (j2 - j) * P
                                mm = pe.matmul(AXf[:, off:off + T - j2 * P], late[:, 3, :], part[:, c2:c2 + T - j2 * P],
                                               start=False, stop=part is spl and j2 == NCH - 1, skip_group_check=True)
                    mm.then_inc(cum_done, 1)

            def values(h):
                p, e = h // 2, h % 2
                pe.wait_ge(w_ready, 2 * h + 2)
                pe.wait_ge(vtok_ready, p + 1)
                if e == 0 and p >= 1:
                    pe.wait_ge(mixl_ready, p)
                for j in range(NCH):
                    c = KCOL[j]
                    mm = pe.matmul(AX[64 * e:64 * e + 64, 3, j * P:T], vtok[:, p % 2, j, 64 * e:64 * e + 64],
                                   pw[:, c:c + T - j * P], start=j == 0, stop=j == NCH - 1, skip_group_check=True)
                mm.then_inc(pv_done, 1)

            def pool_map(g):
                pe.wait_ge(pooled_ready, g + 1)
                if g == 0:
                    pe.wait_ge(s_con, 80)
                pe.wait_ge(vtok_ready, g + 1)
                pe.matmul(PR[:, 2, :], wp[:, g, :], pooled[:, :], start=True, stop=True).then_inc(pooly_done, 1)

            for u in range(4):
                in_unit(u)
            v_turn(0)
            for h in range(HEADS):
                p, e = h // 2, h % 2
                scores(h)
                if p < 3:
                    in_unit(4 * (p + 1) + 2 * e)
                later_keys(h)
                if p < 3:
                    in_unit(4 * (p + 1) + 2 * e + 1)
                if e == 0:
                    pool_map(p)
                else:
                    mod_sum(2 + p)
                values(h)
                if e == 1 and p < 3:
                    v_turn(p + 1)

            pe.wait_ge(mixl_ready, 4)
            pe.wait_ge(pooll_ready, 4)
            pe.wait_ge(mod_ready, 3)
            wait = banks([(mix_ready, R0)] * 4)
            with pe.Fori(0, 2) as i:
                for j in range(4):
                    wait(i, j)
                    unit(4 * i + (U_OUT + j), j, mixh, mixl, 0, KT, PR[:, j, :])
            sum_once(V_OUT + KT)
            sumsq(8)

            def feed_forward(n, first_u, first_dn, hh, hl, ready, fh, fl, gate_taken, up_taken, down_taken):
                wait = banks([gate_taken, up_taken] * 2)
                with pe.Fori(0, FT // 2) as i:
                    for j in range(4):
                        wait(i, j)
                        unit(4 * i + (first_u + j), j, hh, hl, 0, KT, PR[:, j, :],
                             each=ready if j == 0 else None)
                pe.wait_ge(gate_taken[0], R0 + FT - 1)
                pe.wait_ge(up_taken[0], R0 + FT - 1)
                wait = banks([down_taken] * 2, nb=2)
                with pe.Fori(0, KT // 2) as i:
                    for b in range(2):
                        wait(i, b)
                        for j, (k0, nk) in enumerate(DOWN_K):
                            if b == 0:
                                pe.wait_ge(fl_ready, FT * (n - 1) + k0 + nk)
                            unit(8 * i + (first_dn + 4 * b + j), j, fh, fl, k0, nk, PR[:, b, :],
                                 first=j == 0, last=j == 3)

            pe.wait_ge(mix_ready, R0 + 8)
            feed_forward(1, U_GU1, U_DN1, h2h, h2l, lambda k: lo_part(1, k), fh1, fl1, (sg_ready, R0),
                         (ff_ready, R0), (mix_ready, R0 + 8))
            sum_once(V_DN1 + KT)
            sumsq(16)

            wait = banks([(c_ready, R0), (pr_ready, R0), (cv_ready, R0)] * 4)
            with pe.Fori(0, 2) as i:
                for j in range(12):
                    wait(i, j)
                    unit(12 * i + (U_SC + j), j % 4, h3h, h3l, 0, KT, PR[:, j % 4, :],
                         each=(lambda k: lo_part(2, k)) if j == 0 else None)
            pe.wait_ge(cv_ready, R0 + 7)
            wait = banks([(sgb_ready, R0), (mrg_ready, R0)] * 2)
            with pe.Fori(0, 4) as i:
                for j in range(4):
                    wait(i, j)
                    if j == 1:
                        pe.wait_ge(vl_ready, KT)
                    oh, ol = (h3h, h3l) if j % 2 == 0 else (vh, vl)
                    unit(4 * i + (U_SCP + j), j, oh, ol, 0, KT, PR[:, j, :])

            pe.wait_ge(dt_v, 1)
            for c in range(NCH):
                for k in range(KT):
                    for n, (hx, wx) in enumerate(((h3h, wdth), (h3l, wdth), (h3h, wdtl))):
                        mm = pe.matmul(AX[:, 0, 32 * c:32 * c + 32], hx[:, k, c * P:(c + 1) * P], wx[:, k, :],
                                       start=k == 0 and n == 0, stop=k == KT - 1 and n == 2)
            mm.then_inc(dt_done, 1)
            pe.wait_ge(sgb_ready, R0 + 7)
            wait = banks([(xr_ready, R0)] * 4)
            with pe.Fori(0, 2) as i:
                for j in range(4):
                    wait(i, j)
                    if j == 1:
                        pe.wait_ge(mrg_ready, R0 + KT)
                    unit(4 * i + (U_BC + j), j, h3h, h3l, 0, KT, PR[:, j, :])
            pe.wait_ge(dt_v, 6)
            for n, m in enumerate(("upto", "after", "ones")):
                mm = pe.matmul(AX[:, 1, n * P:(n + 1) * P], con_(m), da[:, :, :].rearrange("p c h -> p (c h)"),
                               start=True, stop=True)
            mm.then_inc(acum_done, 1)

            def ssd_first(g, j):
                pe.wait_ge(xs_ready, 4 * g + (j + 1))
                pe.wait_ge(btok_ready, g + 1)
                if j > 0:
                    pe.wait_ge(yo_ready, 4 * g + j)
                for c in range(NCH):
                    mm = pe.transpose(AX[:, 3, c * P:(c + 1) * P], xs[:, j % 2, c * P:(c + 1) * P], con_("ident"))
                mm.then_inc(xtr_done, 1)
                pe.wait_ge(atgl_ready, g + 1)
                if j > 0 or not isinstance(g, int):
                    pe.wait_ge(eab_ready, 4 * g + j)
                if j == 1 and not isinstance(g, int):
                    pe.wait_ge(ln_ready, g + 5)
                for e in range(2):
                    pe.matmul(AX[:, e, :], sel[:, (2 * j + e) * P:(2 * j + e + 1) * P], atg[:, :], start=True, stop=True).then_inc(
                        abc_done, 1)

            def ssd_states(g, j):
                pe.wait_ge(xde_ready, 4 * g + (j + 1))
                for c in range(3):
                    mm = pe.matmul(AX[:, 3, c * P:(c + 1) * P], btok[:, c, :], xde[:, c, :], start=True, stop=True)
                mm.then_inc(stp_done, 1)
                pe.wait_ge(seg_ready, 8 * g + (2 * j + 1))
                pe.matmul(AX[:, 0, :], sel[:, (8 + j % 4) * P:(9 + j % 4) * P], atg[:, :], start=True, stop=True).then_inc(pair_done, 1)

            def ssd_second(g, j):
                if j != 0:
                    pe.wait_ge(yb_ready, 4 * g + j)
                for e in range(2):
                    pe.wait_ge(sc_ready, 8 * g + (2 * j + e + 1))
                    for c in range(NCH):
                        pe.matmul(AX[64 * e:64 * e + 64, 2, c * P:(c + 1) * P], xdt[:, c, 64 * e:64 * e + 64],
                                  seg[:, e, c, :], start=True, stop=True, skip_group_check=True)
                pe.wait_ge(st_step, 20 * g + 5 * (j + 1))
                for c in range(1, NCH):
                    mm = pe.matmul(AX[:, 3, c * P:(c + 1) * P], st[:, c - 1, :], ct[:, c * P:(c + 1) * P],
                                   start=True, stop=True)
                mm.then_inc(y_done, 1)

            wait = banks([(xr_ready, R0 + 8), (sz_ready, R0)] * 4)

            def group_sum(g):
                pe.wait_ge(vacc, 4 * g + V_SSD)
                pe.matmul(AX[:, 1, :], con_("ones"), ssum[:, :], start=True, stop=True).then_inc(ss_ready, 1)

            def group_decays(g):
                pe.wait_ge(grp_ready, 3 * g + 2)
                if isinstance(g, int):
                    pe.wait_ge(atok_ready, 3)
                else:
                    pe.wait_ge(seg_ready, 8 * g)
                for c in range(NCH):
                    mm = pe.matmul(AX[0:8, 1, c * P:(c + 1) * P], dag[:, c, :], con_("upto"), start=True, stop=True,
                                   skip_group_check=True)
                mm.then_inc(atg_done, 1)

            def ssd_group(g):
                later = not isinstance(g, int)
                for j in range(4):
                    for q in range(2):
                        r = 2 * j + q
                        wait(g, r)
                        before = q == 0 and (j > 0 or later)

                        def halfway():
                            ssd_states(g, j - 1)
                            if j == 1 and later:
                                pe.wait_ge(seg_ready, 8 * g + 2)
                                group_sum(g)
                        unit(8 * g + (U_SSD + r), r % 4, h3h, h3l, 0, KT, PR[:, r % 4, :],
                             halfway=halfway if before else None)
                        if before:
                            ssd_second(g, j - 1)
                        if r == (0 if later else 1):
                            group_decays(g)
                    if j == 0:
                        pe.wait_ge(grp_ready, 3 * g + 3)
                        if later:
                            pe.wait_ge(yb_ready, 4 * g)
                        for c in range(NCH):
                            s = slice(c * P, (c + 1) * P)
                            mm = pe.matmul(AX[:, 2, s], bt[:, s], ct[:, s], start=True, stop=True)
                        mm.then_inc(cb_done, 1)
                        if later:
                            pe.wait_ge(yo_ready, 4 * g)
                        for c in range(NCH):
                            s = slice(c * P, (c + 1) * P)
                            mm = pe.transpose(AX[:, 3, s], bt[:, s], con_("ident"))
                        mm.then_inc(btr_done, 1)
                    ssd_first(g, j)
                    if j == 0:
                        pe.wait_ge(cbm_ready, g + 1)

            pe.wait_ge(sel_ready, 1)
            ssd_group(0)
            with pe.Fori(1, GROUPS) as g:
                ssd_group(g)

            wait = banks([(sga_ready, R0), (ta_ready, R0)] * 4)

            def merge(i, m, last_tile=False):
                wait(i, 2 * m)
                unit(12 * i + (U_MRG + 3 * m), (3 * m) % 4, h3h, h3l, 0, KT, PR[:, (2 * m) % 4, :],
                     halfway=(lambda: ssd_states(GROUPS, -1)) if last_tile else None)
                if last_tile:
                    ssd_second(GROUPS, -1)
                    pe.wait_ge(seg_ready, 8 * GROUPS)
                    group_sum(GROUPS)
                    pe.wait_ge(sz_ready, R0 + 16)
                wait(i, 2 * m + 1)
                for q in range(2):
                    unit(12 * i + (U_MRG + 3 * m + 1 + q), (3 * m + 1 + q) % 4, yh, yl, KT * q, KT,
                         PR[:, (2 * m + 1) % 4, :], first=q == 0, last=q == 1,
                         each=(lambda k: (yl_ready, KT * q + k + 1)) if last_tile else None)

            for m in range(8):
                merge(m // 4, m % 4, last_tile=m == 0)
            pe.wait_ge(ml_ready, KT)
            wait = banks([(res_ready, RES_WO)] * 4)
            with pe.Fori(0, 2) as i:
                for j in range(4):
                    wait(i, j)
                    unit(4 * i + (U_WO + j), j, mh, ml, 0, KT, PR[:, j, :])
            sum_once(V_WO + KT)
            feed_forward(2, U_GU2, U_DN2, h4h, h4l, lambda k: (hl_ready, HL_WO + k + 1), fh2, fl2,
                         (gs_ready, R0), (us_ready, R0), (res_ready, RES_WO + KT))
            sum_once(V_DN2 + KT)

        @block.scalar
        def _(act):
            def hi(i, per, c):
                j = c % RING
                if not isinstance(i, int) or per * i + c >= RING:
                    act.wait_ge(unit_used, per * i + (c - RING + 1))
                act.wait_ge(raw_in[j], (per // RING * 16) * i + 16 * (c // RING + 1))
                act.activation(whi[:, j, :], raw[:, j, :], ACT.Copy).then_inc(hi_ready, 1)

            def squares(first, ready=None):
                for k in range(KT):
                    if first + k >= 2:
                        act.wait_ge(sq_used, first + k - 1)
                    if ready is None:
                        act.wait_ge(s_x, 16)
                    else:
                        act.wait_ge(*ready(k))
                    act.activation(sq[:, k % 2, :], x[:, k, :], ACT.Square).then_inc(sq_ready, 1)

            def rms(n, ready, count, width=D, bank=0):
                act.preload_act_table_set("natural_log_exp_and_others")
                act.wait_ge(ready, count)
                act.activation(rr[:, :], AX[:, bank, :], ACT.Ln, bias=vec_("eps", 0), scale=1.0 / width).then_inc(ln_ready, 1)
                act.wait_ge(ln_ready, n)
                act.activation(rr[:, :], rr[:, :], ACT.Exp, scale=-0.5).then_inc(r_ready, 1)

            def split_h(n, ht, hh, shift=None):
                for k in range(KT):
                    act.wait_ge(ht_ready, KT * n + k + 1)
                    if shift is None:
                        ins = act.activation(hh[:, k, :], ht[:, k % RING, :], ACT.Copy)
                    elif k in BY_POOL:
                        act.activation(ht[:, k % RING, :], ht[:, k % RING, :], ACT.Identity, bias=shift(k)).then_inc(
                            hs_ready, 1)
                        act.wait_ge(hs_ready, len(BY_POOL) * n + BY_POOL.index(k) + 1)
                        ins = act.activation(hh[:, k, :], ht[:, k % RING, :], ACT.Copy)
                    else:
                        ins = act.activation(hh[:, k, :], ht[:, k % RING, :], ACT.Identity, bias=shift(k))
                    ins.then_inc(hh_ready, 1)

            for s in (mix_ready, sg_ready, c_ready, sgb_ready, xr_ready, sga_ready):
                act.sem_inc(s, R0)

            act.wait_ge(s_con, 48)
            act.activation(cvec[:, :], vec[:, V["c"]:V["c"] + KT], ACT.Silu).then_inc(cvec_ready, 1)
            squares(0)
            act.activation(late[:, :, :], att[:, :, :], ACT.Copy).then_inc(late_ready, 1)
            rms(1, sq_used, 8)
            for u in range(LEAD):
                hi(0, 4, u)
            split_h(0, ht1, h1h, lambda k: mod[:, k:k + 1])

            def in_result(u):
                p, kind = u // 4, u % 4
                act.wait_ge(unit_used, u + 1)
                if kind == 0:
                    if p >= 2:
                        act.wait_ge(z_done, 4 * p - 4)
                    ins = act.activation(qT[:, p % 2, :], PR[:, u % 2, :], ACT.Copy, scale=0.125)
                elif kind == 1:
                    ins = act.activation(kT[:, p % 2, :], PR[:, u % 2, :], ACT.Copy)
                elif kind == 2:
                    if p >= 1:
                        act.wait_ge(vtr_done, p)
                    ins = act.activation(vT[:, :], PR[:, u % 2, :], ACT.Copy)
                else:
                    if p >= 1:
                        act.wait_ge(pooled_ready, p)
                    else:
                        act.wait_ge(pad_zero, 3)
                    ins = act.activation(padA[:, 16:], PR[:, u % 2, :], ACT.Copy)
                ins.then_inc(qkvu_ready, 1)

            def v_tok(p):
                act.wait_ge(vtr_done, p + 1)
                if p >= 2:
                    act.wait_ge(pv_done, 2 * p - 2)
                act.activation(vtok[:, p % 2, :, :].rearrange("p a b -> p (a b)"), PR[:, 2, :], ACT.Copy).then_inc(
                    vtok_ready, 1)

            def soft(h):
                for n, (c, w, _) in enumerate(PARTS):
                    k, cols = 2 * h + n + 1, slice(c, c + w)
                    act.wait_ge(z_done, k)
                    if h >= 1:
                        act.wait_ge(sp_ready, k - 2)
                    act.activation(az[:, cols], AXf[:, cols], ACT.Abs).then_inc(az_ready, 1)
                    act.wait_ge(az_ready, k)
                    act.activation(az[:, cols], az[:, cols], ACT.Exp, scale=-1.0).then_inc(e_ready, 1)
                    act.wait_ge(e_ready, k)
                    act.activation(az[:, cols], az[:, cols], ACT.Ln, bias=1.0).then_inc(l_ready, 1)
                for n, (c, w, _) in enumerate(PARTS):
                    act.wait_ge(sp_ready, 2 * h + n + 1)
                    if h >= 1:
                        act.wait_ge(cum_done, 2 * h)
                    act.activation(sph[:, c:c + w], sp_[:, c:c + w], ACT.Copy).then_inc(sph_ready, 1)

            def weights(h):
                for n, (c, w, _) in enumerate(PARTS):
                    act.wait_ge(cum_done, 2 * h + n + 1)
                    if h >= 1:
                        act.wait_ge(pv_done, h)
                    act.activation(pw[:, c:c + w], AXf[:, c:c + w], ACT.Exp).then_inc(w_ready, 1)

            def in_step(u):
                hi(0, 4, u + LEAD)
                in_result(u)

            for u in range(4):
                in_step(u)
            v_tok(0)
            for h in range(HEADS):
                p, e = h // 2, h % 2
                soft(h)
                if p < 3:
                    in_step(4 * (p + 1) + 2 * e)
                weights(h)
                if p < 3:
                    in_step(4 * (p + 1) + 2 * e + 1)
                if e == 0:
                    act.wait_ge(pooly_done, p + 1)
                    act.activation(mixh[:, 4 + p, :], PR[:, 2, :], ACT.Copy, scale=vec_("pool_scale", p)).then_inc(
                        poolh_ready, 1)
                else:
                    act.wait_ge(pv_done, h + 1)
                    act.activation(mixh[:, p, :], AX[:, 3, :], ACT.Copy).then_inc(mixh_ready, 1)
                    if p < 3:
                        v_tok(p + 1)

            def keep(sq_slot, bank, dst):
                act.activation(sq[:, sq_slot, :], bank, ACT.Square).then_inc(msq_ready, 1)
                act.activation(dst, bank, ACT.Copy).then_inc(mix_ready, 1)

            with act.Fori(0, 2) as i:
                for j in range(4):
                    hi(i, 4, U_OUT + j + LEAD)
                    act.wait_ge(unit_used, 4 * i + (U_OUT + j + 1))
                    act.wait_ge(vacc, 4 * i + (V_OUT + j))
                    keep(j % 2, PR[:, j, :], tile(mix1, 4 * i + j))
            rms(2, ss_ready, 1)
            squares(8, lambda k: shared(res_ready, res_pool, 0, k))
            rms(3, sq_used, 16)
            split_h(1, ht2, h2h, lambda k: mod[:, 24 + k:25 + k])

            def feed_forward(n, first_u, sg, ff, fh):
                with act.Fori(0, FT // 2) as i:
                    for b in range(2):
                        hi(i, 4, first_u + 2 * b + LEAD)
                        if n == 1:
                            act.wait_ge(unit_used, 4 * i + (first_u + 2 * b + 1))
                            act.activation(sg[:, b, :], PR[:, 2 * b, :], ACT.Silu).then_inc(sg_ready, 1)
                        else:
                            act.wait_ge(gs_ready, 2 * i + (R0 + b + 1))
                            act.activation(sg[:, b, :], sg[:, b, :], ACT.Silu).then_inc(sg_ready, 1)
                        hi(i, 4, first_u + 2 * b + 1 + LEAD)
                        act.wait_ge(ff_ready, 2 * i + (R0 + FT * (n - 1) + b + 1))
                        act.activation(tile(fh, 2 * i + b), ff[:, b, :], ACT.Copy).then_inc(fh_ready, 1)

            feed_forward(1, U_GU1, sg1, ff1, fh1)
            with act.Fori(0, KT // 2) as i:
                for b in range(2):
                    for j in range(4):
                        hi(i, 8, U_DN1 + 4 * b + j + LEAD)
                    act.wait_ge(unit_used, 8 * i + (U_DN1 + 4 * b + 4))
                    act.wait_ge(vacc, 2 * i + (V_DN1 + b))
                    keep(b, PR[:, b, :], tile(mix2, 2 * i + b))
            rms(4, ss_ready, 2)
            squares(16, lambda k: shared(res_ready, res_pool, 1, k))
            rms(5, sq_used, 24)
            split_h(2, ht3, h3h)

            for k in range(KT - RING, KT):
                act.wait_ge(*lo_part(2, k))
            act.wait_ge(s_wdt, 16)
            act.activation(wdth[:, :, :], wdtr[:, :, :], ACT.Copy).then_inc(dt_a, 1)
            with act.Fori(0, 2) as i:
                for m in range(4):
                    for q in range(3):
                        hi(i, 12, U_SC + 3 * m + q + LEAD)
                        if q == 0:
                            act.wait_ge(unit_used, 12 * i + (U_SC + 3 * m + 1))
                            act.activation(cb[:, m % 2, :], PR[:, (3 * m) % 4, :], ACT.Copy).then_inc(c_ready, 1)
                    act.wait_ge(cv_ready, 4 * i + (R0 + m + 1))
                    act.activation(tile(vh, 4 * i + m), cv[:, m % 2, :], ACT.Copy).then_inc(vh_ready, 1)
            with act.Fori(0, 4) as i:
                for j in range(4):
                    hi(i, 4, U_SCP + j + LEAD)
                    if j % 2 == 0:
                        act.wait_ge(unit_used, 4 * i + (U_SCP + j + 1))
                        act.wait_ge(mrg_ready, 2 * i + (R0 + j // 2 - 1))
                        act.activation(sgb[:, j // 2, :], PR[:, j, :], ACT.Sigmoid).then_inc(sgb_ready, 1)
            act.wait_ge(s_con, 80)
            act.activation(sel[:, :], sel_raw[:, :], ACT.Copy).then_inc(sel_ready, 1)
            act.activation(ea[:, :], vec[:, V["a_log"]:V["a_log"] + 32], ACT.Exp).then_inc(dt_a, 1)
            act.preload_act_table_set("natural_log_exp_and_others")
            act.wait_ge(dt_v, 4)
            act.activation(dte[:, :, :], dte[:, :, :], ACT.Exp).then_inc(dt_a, 1)
            act.wait_ge(dt_a, 3)
            act.activation(dte[:, :, :], dte[:, :, :], ACT.Ln, bias=1.0).then_inc(dt_a, 1)
            act.wait_ge(pad_zero, 5)
            with act.Fori(0, 2) as i:
                for j in range(4):
                    hi(i, 4, U_BC + j + LEAD)
                    act.wait_ge(unit_used, 4 * i + (U_BC + j + 1))
                    act.activation(xr[:, j % 2, 3:], PR[:, j, :], ACT.Copy).then_inc(xr_ready, 1)
                    act.wait_ge(conv_ready, 4 * i + (j + 1))
                    act.activation(tile(bc, 4 * i + j), cx[:, j % 2, :], ACT.Silu).then_inc(bc_ready, 1)
            act.wait_ge(acum_done, 1)
            for n, (dst, f) in enumerate(((atok, ACT.Copy), (toend, ACT.Exp), (dec, ACT.Exp))):
                act.activation(dst[:, :, :].rearrange("p c h -> p (c h)"), AX[:, 1, n * P:(n + 1) * P], f).then_inc(
                    atok_ready, 1)

            def v_square(g, j):
                act.wait_ge(yv_ready, 4 * g + (j + 1))
                act.wait_ge(vacc, 4 * g + (V_SSD - 1 + j))
                act.activation(sq[:, j % 2, :], tile(yy, 4 * g + j), ACT.Square).then_inc(vsq_ready, 1)

            def decays(g):
                act.wait_ge(atg_done, g + 1)
                if not isinstance(g, int):
                    act.wait_ge(pair_done, 4 * g)
                else:
                    act.wait_ge(pad_zero, 6)
                act.activation(atg[0:8, :], AX[0:8, 1, :], ACT.Copy).then_inc(atg_ready, 1)

            def ssd_group(g):
                later = not isinstance(g, int)
                for j in range(4):
                    hi(g, 8, U_SSD + 2 * j + LEAD)
                    act.wait_ge(unit_used, 8 * g + (U_SSD + 2 * j + 1))
                    act.activation(xr[:, j % 2, 3:], PR[:, (2 * j) % 4, :], ACT.Copy).then_inc(xr_ready, 1)
                    if j == 0 and later:
                        decays(g)
                    act.wait_ge(conv_ready, 4 * g + (9 + j))
                    act.activation(th[:, :], cx[:, j % 2, :], ACT.Tanh, scale=0.5).then_inc(th_ready, 1)
                    if j == 1 and later:
                        rms(g + 5, ss_ready, g + 2, width=4 * 512, bank=1)
                    hi(g, 8, U_SSD + 2 * j + 1 + LEAD)
                    if j > 0 or later:
                        v_square(g, j - 1)
                    act.wait_ge(unit_used, 8 * g + (U_SSD + 2 * j + 2))
                    act.activation(gz[:, :], PR[:, (2 * j + 1) % 4, :], ACT.Tanh, scale=0.5).then_inc(thz_ready, 1)
                    if j == 0 and not later:
                        decays(g)
                    if j == 0:
                        act.wait_ge(btr_done, g + 1)
                        act.activation(btok[:, :, :].rearrange("p a b -> p (a b)"), AX[:, 3, :], ACT.Copy).then_inc(
                            btok_ready, 1)
                    for e in range(2):
                        act.wait_ge(seg_ready, 8 * g + (2 * j + e + 1))
                        act.activation(seg[:, e, :, :], seg[:, e, :, :], ACT.Exp).then_inc(ex_ready, 1)
                    act.wait_ge(pair_done, 4 * g + (j + 1))
                    act.activation(eab[:, :], AX[:, 0, :], ACT.Exp).then_inc(eab_ready, 1)

            ssd_group(0)
            with act.Fori(1, GROUPS) as g:
                ssd_group(g)
            v_square(GROUPS, -1)

            for k in range(16):
                if k == 5:
                    rms(GROUPS + 5, ss_ready, GROUPS + 2, width=4 * 512, bank=1)
                act.wait_ge(yy_ready, k + 1 if k < 12 else 16)
                act.activation(yh[:, k, :], yy[:, k, :], ACT.Copy).then_inc(yh_ready, 1)
            with act.Fori(0, 2) as i:
                for m in range(4):
                    for q in range(3):
                        hi(i, 12, U_MRG + 3 * m + q + LEAD)
                        if q == 0:
                            act.wait_ge(unit_used, 12 * i + (U_MRG + 3 * m + 1))
                            act.activation(sga[:, m % 2, :], PR[:, (2 * m) % 4, :], ACT.Sigmoid).then_inc(sga_ready, 1)
                    act.wait_ge(mrg_ready, 4 * i + (R0 + 9 + m))
                    act.activation(tile(mh, 4 * i + m), tile(mrg, 4 * i + m), ACT.Copy).then_inc(mh_ready, 1)
            def x_square(i, per, c, v0):
                act.wait_ge(res_ready, per * i + (c + RES_WO + (KT if v0 == V_DN2 else 0) + 1))
                act.wait_ge(vacc, per * i + (v0 + c))
                act.activation(sq[:, c % 2, :], tile(x, per * i + c), ACT.Square).then_inc(msq_ready, 1)

            with act.Fori(0, 2) as i:
                for j in range(4):
                    hi(i, 4, U_WO + j + LEAD)
                    x_square(i, 4, j, V_WO)
                    act.wait_ge(ht_ready, 4 * i + (24 + j + 1))
                    act.activation(tile(h4h, 4 * i + j), ht4[:, j, :], ACT.Copy).then_inc(hh_ready, 1)
            rms(10, ss_ready, 7)
            feed_forward(2, U_GU2, sg2, ff2, fh2)
            def down_tile(i, b):
                for j in range(4):
                    c = U_DN2 + 4 * b + j + LEAD
                    if not isinstance(i, int) or 8 * i + c < U_END:
                        hi(i, 8, c)
                x_square(i, 2, b, V_DN2)

            with act.Fori(0, 3) as i:
                down_tile(i, 0)
                down_tile(i, 1)
            down_tile(3, 0)
            down_tile(3, 1)
            rms(11, ss_ready, 8)

        @block.vector
        def _(dve):
            counts = {"upd": 0, "pool": 0}

            def cols(name, k=0, n=KT):
                return vec[:, V[name] + k:V[name] + k + n]

            def make_h(n_r, n, scale, shift, ht, hh, hl):
                dve.wait_ge(r_ready, n_r)

                def full(k):
                    if k >= RING:
                        dve.wait_ge(*lo_part(n, k - RING))
                    dve.scalar_tensor_tensor(ht[:, k % RING, :], x[:, k, :], scale(k), rr[:, :], ALU.mult,
                                             ALU.mult).then_inc(ht_ready, 1)

                full(0)
                for k in range(KT):
                    if k + 1 < KT:
                        full(k + 1)
                    if k in BY_POOL:
                        continue
                    dve.wait_ge(hh_ready, KT * n + k + 1)
                    if shift is None:
                        ins = dve.tensor_tensor(hl[:, k, :], ht[:, k % RING, :], hh[:, k, :], ALU.subtract)
                    else:
                        ins = dve.scalar_tensor_tensor(hl[:, k, :], ht[:, k % RING, :], shift(k), hh[:, k, :], ALU.add,
                                                       ALU.subtract)
                    ins.then_inc(hl_ready, 1)

            def mod_unit(n):
                m, k = n // KT, n % KT
                dve.wait_ge(cond_in[n % RING], 16 * (n // RING + 1))
                if k == 0:
                    if m >= 2:
                        dve.wait_ge(msum_done, m - 1)
                    ins = dve.tensor_scalar(macc[:, m % 2, :], cond[:, n % RING, :], cvec[:, k:k + 1], None, ALU.mult)
                else:
                    dve.wait_ge(cond_used, n)
                    ins = dve.scalar_tensor_tensor(macc[:, m % 2, :], cond[:, n % RING, :], cvec[:, k:k + 1],
                                                   macc[:, m % 2, :], ALU.mult, ALU.add)
                ins.then_inc(cond_used, 1)

            for s in (gs_ready, us_ready, ff_ready, pr_ready, cv_ready, mrg_ready, sz_ready, ta_ready):
                dve.sem_inc(s, R0)

            for m in (padA, padB, padC):
                dve.memset(m[:, 0:16], 0.0).then_inc(pad_zero, 1)
            dve.wait_ge(cvec_ready, 1)
            for n in range(16):
                mod_unit(n)
            dve.wait_ge(msum_done, 2)
            dve.tensor_tensor(mod[:, 0:16], PR[:, 3, 0:16], cols("b_cond", 0, 16), ALU.add).then_inc(mod_ready, 1)
            dve.wait_ge(mod_ready, 1)
            dve.scalar_tensor_tensor(amix[:, :], mod[:, 8:16], 1.0, cols("g_mix_pre"), ALU.add, ALU.mult).then_inc(
                mod_ready, 1)
            dve.wait_ge(mod_ready, 2)
            dve.wait_ge(s_x, 16)
            make_h(1, 0, lambda k: amix[:, k:k + 1], lambda k: mod[:, k:k + 1], ht1, h1h, h1l)

            def soft_plus(h):
                for n, (c, w, _) in enumerate(PARTS):
                    dve.wait_ge(l_ready, 2 * h + n + 1)
                    if h >= 1:
                        dve.wait_ge(cum_done, 2 * h)
                    dve.scalar_tensor_tensor(sp_[:, c:c + w], AXf[:, c:c + w], 0.0, az[:, c:c + w], ALU.max,
                                             ALU.add).then_inc(sp_ready, 1)
                for n, (c, w, _) in enumerate(PARTS):
                    dve.wait_ge(sph_ready, 2 * h + n + 1)
                    dve.tensor_tensor(spl[:, c:c + w], sp_[:, c:c + w], sph[:, c:c + w], ALU.subtract).then_inc(
                        spl_ready, 1)

            def pool_step(ins):
                counts["pool"] += 1
                ins.then_inc(pstep, 1)

            def pooling(g):
                dve.wait_ge(qkvu_ready, 4 * g + 4)
                src = padA
                for s in range(g + 1):
                    dst, w = (padB, padC)[s % 2], 1 << s
                    pool_step(dve.tensor_tensor(dst[:, 16:], src[:, 16:], src[:, 16 - w:16 - w + T], ALU.add))
                    dve.wait_ge(pstep, counts["pool"])
                    src = dst
                if g >= 1:
                    dve.wait_ge(pooly_done, g)
                pool_step(dve.scalar_tensor_tensor(pooled[:, :], src[:, 16:], 1.0 / (2 << g), padA[:, 16:], ALU.mult,
                                                   ALU.subtract))
                pool_step(dve.tensor_tensor(pfix[:, :], src[:, 16:32], con_("inv", 16 * g, 16), ALU.mult))
                dve.wait_ge(pstep, counts["pool"])
                dve.tensor_tensor(pooled[:, 0:16], pfix[:, :], padA[:, 16:32], ALU.subtract).then_inc(pooled_ready, 1)

            def pool_low(g):
                dve.wait_ge(poolh_ready, g + 1)
                dve.scalar_tensor_tensor(mixl[:, 4 + g, :], PR[:, 2, :], vec_("pool_scale", g), mixh[:, 4 + g, :],
                                         ALU.mult, ALU.subtract).then_inc(pooll_ready, 1)

            for h in range(HEADS):
                p, e = h // 2, h % 2
                for n in range(16 + 4 * h, 18 + 4 * h):
                    mod_unit(n)
                soft_plus(h)
                for n in range(18 + 4 * h, 20 + 4 * h):
                    mod_unit(n)
                if e == 0:
                    pooling(p)
                if e == 0:
                    pool_low(p)
                else:
                    dve.wait_ge(mixh_ready, p + 1)
                    dve.tensor_tensor(mixl[:, p, :], AX[:, 3, :], mixh[:, p, :], ALU.subtract).then_inc(mixl_ready, 1)

            dve.wait_ge(msum_done, 6)
            dve.tensor_tensor(mod[:, 16:48], PR[:, 3, 16:48], cols("b_cond", 16, 32), ALU.add).then_inc(mod_ready, 1)

            def accumulate(i, per, c, slot, first, v0):
                dve.wait_ge(msq_ready, per * i + (first + c + 1))
                dve.wait_ge(vacc, per * i + (v0 + c))
                dve.tensor_tensor(ssum[:, :], ssum[:, :], sq[:, slot, :], ALU.add).then_inc(vacc, 1)

            def post_norm(n_r, mix, gate):
                dve.wait_ge(r_ready, n_r)

                def residual(k, updates):
                    if k not in BY_POOL:
                        dve.wait_ge(upd_ready, updates)
                        dve.tensor_tensor(x[:, k, :], x[:, k, :], mix[:, k, :], ALU.add).then_inc(res_ready, 1)

                for k in range(KT):
                    dve.scalar_tensor_tensor(mix[:, k, :], mix[:, k, :], gate[:, k:k + 1], rr[:, :], ALU.mult,
                                             ALU.mult).then_inc(upd_ready, 1)
                    counts["upd"] += 1
                    if k > 0:
                        residual(k - 1, counts["upd"] - 1)
                residual(KT - 1, counts["upd"])

            dve.memset(ssum[:, :], 0.0).then_inc(vacc, 1)
            with dve.Fori(0, 2) as i:
                for j in range(4):
                    accumulate(i, 4, j, j % 2, 0, V_OUT)
            dve.wait_ge(mod_ready, 3)
            dve.tensor_tensor(gmix[:, :], mod[:, 16:24], cols("g_mix_post"), ALU.mult).then_inc(mod_ready, 1)
            dve.scalar_tensor_tensor(affn[:, :], mod[:, 32:40], 1.0, cols("g_ffn_pre"), ALU.add, ALU.mult).then_inc(
                mod_ready, 1)
            dve.tensor_tensor(gffn[:, :], mod[:, 40:48], cols("g_ffn_post"), ALU.mult).then_inc(mod_ready, 1)
            dve.wait_ge(mod_ready, 6)
            post_norm(2, mix1, gmix)
            make_h(3, 1, lambda k: affn[:, k:k + 1], lambda k: mod[:, 24 + k:25 + k], ht2, h2h, h2l)

            def feed_forward(n, first_u, sg, ff, fh, fl):
                done = FT * (n - 1)
                with dve.Fori(0, FT // 2) as i:
                    for b in range(2):
                        if n == 1:
                            dve.wait_ge(sg_ready, 2 * i + (R0 + done + b + 1))
                            dve.wait_ge(unit_used, 4 * i + (first_u + 2 * b + 2))
                            dve.tensor_tensor(ff[:, b, :], sg[:, b, :], PR[:, 2 * b + 1, :], ALU.mult).then_inc(ff_ready, 1)
                        else:
                            dve.wait_ge(unit_used, 4 * i + (first_u + 2 * b + 1))
                            dve.wait_ge(ff_ready, 2 * i + (R0 + done + b - 1))
                            dve.wait_ge(fl_ready, 2 * i + (done + b - 1))
                            dve.tensor_tensor(sg[:, b, :], PR[:, 2 * b, :], rr[:, :], ALU.mult).then_inc(gs_ready, 1)
                            dve.wait_ge(unit_used, 4 * i + (first_u + 2 * b + 2))
                            dve.tensor_tensor(ff[:, b, :], PR[:, 2 * b + 1, :], rr[:, :], ALU.mult).then_inc(us_ready, 1)
                            dve.wait_ge(sg_ready, 2 * i + (R0 + done + b + 1))
                            dve.wait_ge(us_ready, 2 * i + (R0 + b + 1))
                            dve.tensor_tensor(ff[:, b, :], ff[:, b, :], sg[:, b, :], ALU.mult).then_inc(ff_ready, 1)
                        dve.wait_ge(fh_ready, 2 * i + (done + b + 1))
                        dve.tensor_tensor(tile(fl, 2 * i + b), ff[:, b, :], tile(fh, 2 * i + b), ALU.subtract).then_inc(
                            fl_ready, 1)

            feed_forward(1, U_GU1, sg1, ff1, fh1, fl1)
            dve.memset(ssum[:, :], 0.0).then_inc(vacc, 1)
            with dve.Fori(0, KT // 2) as i:
                for b in range(2):
                    accumulate(i, 2, b, b, 8, V_DN1)
            post_norm(4, mix2, gffn)
            make_h(5, 2, lambda k: cols("norm_mix_w_2", k, 1), None, ht3, h3h, h3l)

            dve.memset(pr[:, :, 0:2], 0.0).then_inc(pad_zero, 1)
            dve.wait_ge(dt_a, 1)
            dve.tensor_tensor(wdtl[:, :, :], wdtr[:, :, :], wdth[:, :, :], ALU.subtract).then_inc(dt_v, 1)
            with dve.Fori(0, 2) as i:
                for m in range(4):
                    dve.wait_ge(c_ready, 4 * i + (R0 + m + 1))
                    dve.wait_ge(unit_used, 12 * i + (U_SC + 3 * m + 2))
                    if m == 0:
                        dve.wait_ge(pad_zero, 4)
                    q = m % 2
                    dve.tensor_tensor(pr[:, q, 2:], cb[:, q, :], PR[:, (3 * m + 1) % 4, :], ALU.mult).then_inc(pr_ready, 1)
                    dve.wait_ge(pr_ready, 4 * i + (R0 + m + 1))
                    dve.tensor_scalar(cv[:, q, :], pr[:, q, 0:T], vec_("sconv_w", 4 * i + m), None, ALU.mult).then_inc(
                        cstep, 1)
                    for k in (1, 2):
                        dve.wait_ge(cstep, 12 * i + (3 * m + k))
                        dve.scalar_tensor_tensor(cv[:, q, :], pr[:, q, k:k + T], vec_("sconv_w", 4 * i + (m + 8 * k)),
                                                 cv[:, q, :], ALU.mult, ALU.add).then_inc(cstep, 1)
                    dve.wait_ge(cstep, 12 * i + (3 * m + 3))
                    dve.wait_ge(unit_used, 12 * i + (U_SC + 3 * m + 3))
                    dve.tensor_tensor(cv[:, q, :], cv[:, q, :], PR[:, (3 * m + 2) % 4, :], ALU.mult).then_inc(cv_ready, 1)
                    dve.wait_ge(vh_ready, 4 * i + (m + 1))
                    dve.tensor_tensor(tile(vl, 4 * i + m), cv[:, q, :], tile(vh, 4 * i + m), ALU.subtract).then_inc(
                        vl_ready, 1)
            with dve.Fori(0, 4) as i:
                for b in range(2):
                    dve.wait_ge(sgb_ready, 2 * i + (R0 + b + 1))
                    dve.wait_ge(unit_used, 4 * i + (U_SCP + 2 * b + 2))
                    dve.tensor_tensor(tile(mrg, 2 * i + b), sgb[:, b, :], PR[:, 2 * b + 1, :], ALU.mult).then_inc(
                        mrg_ready, 1)

            def conv4(i, per, c, chan, slot):
                dve.wait_ge(xr_ready, per * i + (R0 + c + 1))
                dve.tensor_scalar(cx[:, slot, :], xr[:, slot, 0:T], vec_("conv_w", 4 * i + chan),
                                  vec_("conv_b", 4 * i + chan), ALU.mult, ALU.add).then_inc(tap, 1)
                for k in (1, 2, 3):
                    dve.wait_ge(tap, 3 * per * i + (3 * c + k))
                    dve.scalar_tensor_tensor(cx[:, slot, :], xr[:, slot, k:k + T], vec_("conv_w", 4 * i + (chan + 24 * k)),
                                             cx[:, slot, :], ALU.mult, ALU.add).then_inc(tap if k < 3 else conv_ready, 1)

            dve.wait_ge(dt_done, 1)
            dve.tensor_tensor(dta[:, :, :], AX[:, 0, 0:P].rearrange("p (c h) -> p c h", c=NCH),
                              cols("dt_bias", 0, 32).unsqueeze(1).broadcast_to([P, NCH, 32]), ALU.add).then_inc(dt_v, 1)
            dve.wait_ge(dt_v, 2)
            dve.tensor_scalar(dte[:, :, :], dta[:, :, :], 0.0, None, ALU.max).then_inc(dt_v, 1)
            dve.wait_ge(dt_v, 3)
            dve.scalar_tensor_tensor(dte[:, :, :], dte[:, :, :], -2.0, dta[:, :, :], ALU.mult, ALU.add).then_inc(dt_v, 1)
            dve.wait_ge(dt_a, 4)
            dve.scalar_tensor_tensor(dt[:, :, :], dta[:, :, :], 0.0, dte[:, :, :], ALU.max, ALU.add).then_inc(dt_v, 1)
            dve.wait_ge(dt_v, 5)
            dve.scalar_tensor_tensor(da[:, :, :], dt[:, :, :], -1.0, ea[:, :].unsqueeze(1).broadcast_to([P, NCH, 32]),
                                     ALU.mult, ALU.mult).then_inc(dt_v, 1)
            dve.tensor_scalar(dte[:, :, :], dt[:, :, :], 0.5, None, ALU.mult).then_inc(dt_v, 1)
            dve.tensor_scalar(halves[:, 0:16], cols("ssd_norm_w_2", 0, 16), 0.5, None, ALU.mult).then_inc(dt_v, 1)
            dve.tensor_scalar(halves[:, 16:32], cols("d_skip", 0, 16), 0.5, None, ALU.mult).then_inc(dt_v, 1)
            dve.memset(xr[:, :, 0:3], 0.0).then_inc(pad_zero, 1)
            dve.wait_ge(pad_zero, 5)
            with dve.Fori(0, 2) as i:
                for j in range(4):
                    conv4(i, 4, j, 16 + j, j % 2)

            dve.wait_ge(dt_v, 9)
            dve.wait_ge(atok_ready, 3)
            dve.wait_ge(bc_ready, 8)
            dve.memset(atg[:, :].bitcast(F32), 0.0).then_inc(pad_zero, 1)

            def heads(t, g, j, c0=0, c1=NCH, e0=0, n=2):
                return t[:, c0:c1, bass.ds(8 * g + (2 * j + e0), n)]

            def gate(g, j):
                dve.wait_ge(thz_ready, 4 * g + (j + 1))
                dve.scalar_tensor_tensor(gz[:, :], gz[:, :], 1.0, PR[:, (2 * j + 1) % 4, :], ALU.add, ALU.mult).then_inc(
                    sz_ready, 1)

            def gated(g, j):
                dve.wait_ge(y_done, 4 * g + (j + 1))
                dve.scalar_tensor_tensor(yb[:, :], xs[:, j % 2, :], halves[:, bass.ds(4 * g + (16 + j), 1)], AX[:, 2, :],
                                         ALU.mult, ALU.add).then_inc(yb_ready, 1)
                dve.wait_ge(eab_ready, 4 * g + (j + 1))
                dve.tensor_tensor(eab[:, P:], eab[:, P:], AX[:, 3, P:], ALU.mult).then_inc(yo_ready, 1)
                dve.wait_ge(yb_ready, 4 * g + (j + 1))
                dve.wait_ge(yo_ready, 4 * g + (j + 1))
                dve.tensor_tensor(yb[:, P:], yb[:, P:], eab[:, P:], ALU.add).then_inc(y2_ready, 1)
                dve.wait_ge(sz_ready, 4 * g + (R0 + j + 1))
                dve.wait_ge(y2_ready, 4 * g + (j + 1))
                dve.tensor_tensor(tile(yy, 4 * g + j), yb[:, :], gz[:, :], ALU.mult).then_inc(yv_ready, 1)

            def add_square(g, j):
                dve.wait_ge(vsq_ready, 4 * g + (j + 1))
                if j == 0:
                    if not isinstance(g, int):
                        dve.wait_ge(ss_ready, g + 2)
                    dve.tensor_copy(ssum[:, :], sq[:, 0, :]).then_inc(vacc, 1)
                else:
                    dve.wait_ge(vacc, 4 * g + (V_SSD + j))
                    dve.tensor_tensor(ssum[:, :], ssum[:, :], sq[:, j % 2, :], ALU.add).then_inc(vacc, 1)

            def norm_group(g, tiles=(-4, -3, -2, -1)):
                dve.wait_ge(r_ready, g + 5)
                for k in tiles:
                    dve.scalar_tensor_tensor(tile(yy, 4 * g + k), tile(yy, 4 * g + k), halves[:, bass.ds(4 * g + k, 1)],
                                             rr[:, :], ALU.mult, ALU.mult).then_inc(yy_ready, 1)

            def ssd_group(g):
                later = not isinstance(g, int)
                dve.tensor_copy(bt[:, :], tile(bc, g)).then_inc(grp_ready, 1)
                dve.tensor_copy(dag[:, :, :], da[:, :, bass.ds(8 * g, 8)]).then_inc(grp_ready, 1)
                if not later:
                    dve.tensor_copy(ct[:, :], tile(bc, g + 4)).then_inc(grp_ready, 1)
                for j in range(4):
                    conv4(g, 4, 8 + j, j, j % 2)
                    if j > 0 or later:
                        gate(g, j - 1)
                    dve.wait_ge(th_ready, 4 * g + (j + 1))
                    dve.scalar_tensor_tensor(xs[:, j % 2, :], th[:, :], 1.0, cx[:, j % 2, :], ALU.add, ALU.mult).then_inc(
                        xs_ready, 1)
                    if j > 0 or later:
                        gated(g, j - 1)
                    if j == 0 and later:
                        dve.tensor_copy(ct[:, :], tile(bc, g + 4)).then_inc(grp_ready, 1)
                    if j == 0:
                        dve.wait_ge(atg_ready, g + 1)
                        dve.tensor_tensor(atg[32:40, :], AX[0:8, 1, :], atg[0:8, :], ALU.subtract).then_inc(atgl_ready, 1)
                    if j == 0:
                        if later:
                            add_square(g, -1)
                        dve.wait_ge(cb_done, g + 1)
                        dve.tensor_tensor(cbm[:, :, :], AX[:, 2, :].rearrange("p (c l) -> p c l", c=NCH),
                                          con_("upto").unsqueeze(1).broadcast_to([P, NCH, P]), ALU.mult).then_inc(
                                              cbm_ready, 1)
                    dve.wait_ge(xtr_done, 4 * g + (j + 1))
                    dve.tensor_tensor(xdt[:, :, :].rearrange("p c (e d) -> p c e d", e=2),
                                      AX[:, 3, :].rearrange("p (c e d) -> p c e d", c=NCH, e=2),
                                      spread(heads(dte, g, j), [P, NCH, 2, 64]), ALU.mult).then_inc(xdt_ready, 1)
                    dve.wait_ge(xdt_ready, 4 * g + (j + 1))
                    dve.tensor_tensor(xde[:, :, :].rearrange("p c (e d) -> p c e d", e=2),
                                      xdt[:, 0:3, :].rearrange("p c (e d) -> p c e d", e=2),
                                      spread(heads(toend, g, j, 0, 3), [P, 3, 2, 64]), ALU.mult).then_inc(xde_ready, 1)
                    for e in range(2):
                        dve.wait_ge(abc_done, 8 * g + (2 * j + e + 1))
                        for c in range(NCH):
                            ins = dve.tensor_scalar(seg[:, e, c, :], AX[:, e, c * P:(c + 1) * P],
                                                    atok[:, c, bass.ds(8 * g + (2 * j + e), 1)], 0.0, ALU.subtract,
                                                    ALU.min)
                        ins.then_inc(seg_ready, 1)
                    if j > 0:
                        add_square(g, j - 1)
                    dve.wait_ge(stp_done, 4 * g + (j + 1))
                    dve.tensor_copy(st[:, 0, :], AX[:, 3, 0:P]).then_inc(st_step, 1)
                    for c in (1, 2):
                        dve.wait_ge(st_step, 20 * g + (5 * j + 2 * c - 1))
                        dve.tensor_tensor(st[:, c, :].rearrange("p (e d) -> p e d", e=2),
                                          st[:, c - 1, :].rearrange("p (e d) -> p e d", e=2),
                                          spread(heads(dec, g, j, c, c + 1).rearrange("p c e -> p (c e)"), [P, 2, 64]),
                                          ALU.mult).then_inc(st_step, 1)
                        dve.wait_ge(st_step, 20 * g + (5 * j + 2 * c))
                        dve.tensor_tensor(st[:, c, :], st[:, c, :], AX[:, 3, c * P:(c + 1) * P], ALU.add).then_inc(
                            st_step, 1)
                    for e in range(2):
                        dve.wait_ge(ex_ready, 8 * g + (2 * j + e + 1))
                        dve.tensor_tensor(seg[:, e, :, :], seg[:, e, :, :], cbm[:, :, :], ALU.mult).then_inc(sc_ready, 1)
                    if j in (1, 2) and later:
                        norm_group(g, (-4, -3) if j == 1 else (-2, -1))

            ssd_group(0)
            with dve.Fori(1, GROUPS) as g:
                ssd_group(g)
            gate(GROUPS, -1)
            gated(GROUPS, -1)
            add_square(GROUPS, -1)

            for k in range(16):
                if k == 4:
                    norm_group(GROUPS)
                dve.wait_ge(yh_ready, k + 1)
                dve.tensor_tensor(yl[:, k, :], yy[:, k, :], yh[:, k, :], ALU.subtract).then_inc(yl_ready, 1)
            with dve.Fori(0, 2) as i:
                for m in range(4):
                    dve.wait_ge(sga_ready, 4 * i + (R0 + m + 1))
                    dve.wait_ge(unit_used, 12 * i + (U_MRG + 3 * m + 3))
                    dve.tensor_tensor(ta[:, m % 2, :], sga[:, m % 2, :], PR[:, (2 * m + 1) % 4, :], ALU.mult).then_inc(
                        ta_ready, 1)
                    dve.wait_ge(ta_ready, 4 * i + (R0 + m + 1))
                    dve.tensor_tensor(tile(mrg, 4 * i + m), tile(mrg, 4 * i + m), ta[:, m % 2, :], ALU.add).then_inc(
                        mrg_ready, 1)
                    dve.wait_ge(mh_ready, 4 * i + (m + 1))
                    dve.tensor_tensor(tile(ml, 4 * i + m), tile(mrg, 4 * i + m), tile(mh, 4 * i + m),
                                      ALU.subtract).then_inc(ml_ready, 1)
            dve.memset(ssum[:, :], 0.0).then_inc(vacc, 1)
            with dve.Fori(0, 2) as i:
                for j in range(4):
                    dve.wait_ge(unit_used, 4 * i + (U_WO + j + 1))
                    dve.tensor_tensor(tile(x, 4 * i + j), tile(x, 4 * i + j), PR[:, j, :], ALU.add).then_inc(res_ready, 1)
                    dve.wait_ge(res_ready, 4 * i + (RES_WO + j + 1))
                    dve.wait_ge(hl_ready, 4 * i + (HL_WO + j - 3))
                    dve.tensor_scalar(ht4[:, j, :], tile(x, 4 * i + j), vec_("norm_ffn_w_2", 4 * i + j), None,
                                      ALU.mult).then_inc(ht_ready, 1)
                    accumulate(i, 4, j, j % 2, 16, V_WO)
                    dve.wait_ge(hh_ready, 4 * i + (24 + j + 1))
                    dve.wait_ge(ht_ready, 4 * i + (24 + j + 1))
                    dve.tensor_tensor(tile(h4l, 4 * i + j), ht4[:, j, :], tile(h4h, 4 * i + j), ALU.subtract).then_inc(
                        hl_ready, 1)
            dve.wait_ge(r_ready, 10)
            feed_forward(2, U_GU2, sg2, ff2, fh2, fl2)
            dve.memset(ssum[:, :], 0.0).then_inc(vacc, 1)
            with dve.Fori(0, KT // 2) as i:
                for b in range(2):
                    dve.wait_ge(unit_used, 8 * i + (U_DN2 + 4 * b + 4))
                    dve.tensor_tensor(tile(x, 2 * i + b), tile(x, 2 * i + b), PR[:, b, :], ALU.add).then_inc(res_ready, 1)
                    accumulate(i, 2, b, b, 24, V_DN2)
            dve.wait_ge(r_ready, 11)
            for k in range(KT):
                dve.scalar_tensor_tensor(outT[:, k, :], x[:, k, :], cols("final_norm_w_2", k, 1), rr[:, :], ALU.mult,
                                         ALU.mult).then_inc(out_ready, 1)


def kernel(**inputs):
    import numpy as np
    import concourse.bacc as bacc
    from concourse.bass_utils import run_bass_kernel_spmd

    a = {k: np.asarray(v) for k, v in inputs.items()}

    def tiles(w):
        k, n = w.shape
        return w.reshape(k // P, P, n // P, P).transpose(2, 1, 0, 3).reshape(n // P, P, k)

    def paired(*ws):
        return [b for bs in zip(*ws) for b in bs]

    w_in, w2 = tiles(a["w_in"][0]), a["w_in_2"][0]
    z, xs, b_, c_ = (tiles(w2[:, s:s + n]) for s, n in ((0, 2048), (2048, 2048), (4096, 512), (4608, 512)))
    s_b, s_c, s_x, g_a, g_b = (tiles(w2[:, s:s + 1024]) for s in range(5152, 10272, 1024))
    ssd = tiles(a["w_ssd_proj_2"][0]).reshape(8, P, 2, 1024)
    w8 = np.stack(
        [w_in[4 * kind + p] for p in range(4) for kind in range(4)]
        + list(tiles(a["w_out"][0]))
        + paired(tiles(a["w_gate"][0]), tiles(a["w_up"][0]))
        + paired(s_c, s_x, s_b)
        + paired(g_b, tiles(a["w_sconv_proj_2"][0]))
        + list(b_) + list(c_)
        + paired(xs, z)
        + paired(g_a, ssd[:, :, 0], ssd[:, :, 1])
        + list(tiles(a["w_o_2"][0]))
        + paired(tiles(a["w_gate_2"][0]), tiles(a["w_up_2"][0])))
    w22 = np.concatenate([tiles(a["w_down"][0]), tiles(a["w_down_2"][0])])
    wcond = a["w_cond"][0].reshape(KT, P, 6, D).transpose(2, 0, 1, 3).reshape(6 * KT, P, D)
    wdt = np.ascontiguousarray(w2[:, 5120:5152].reshape(KT, P, 32).transpose(1, 0, 2))
    wpool = np.ascontiguousarray(a["w_pool"][0].transpose(1, 0, 2))

    def column(v):
        return np.asarray(v).reshape(-1, P).T

    cols = [column(a["c"]), column(a["b_cond"]), column(a["g_mix_pre"]), column(a["g_mix_post"]), column(a["g_ffn_pre"]),
            column(a["g_ffn_post"]), column(a["pool_scale"]), column(a["norm_mix_w_2"]), column(a["ssd_conv_w_2"]),
            column(a["ssd_conv_b_2"]), column(a["ssd_norm_w_2"]), column(a["sconv_w_2"]), column(a["norm_ffn_w_2"]),
            column(a["final_norm_w_2"]), column(np.repeat(a["d_skip_2"][0], 64)),
            np.repeat(a["dt_bias_2"], P, axis=0), np.repeat(a["a_log_2"], P, axis=0),
            np.full((P, 1), EPS, np.float32)]
    vecs = np.ascontiguousarray(np.concatenate(cols, axis=1))
    assert vecs.shape == (P, NV)

    i, j = np.arange(P)[:, None], np.arange(P)[None, :]
    inv = np.concatenate([1.0 / np.minimum(np.arange(1, 17), 2 << g) for g in range(4)])[None, :].repeat(P, 0)
    atts = np.stack([i == j, np.where(i >= j, -2.0 ** 100, 0.0), -1.0 * (i >= j), -np.ones((P, P))], axis=1).astype(np.float32)
    q, row = np.arange(8 * P)[None, :], np.arange(40)[:, None]
    row = np.where((row < 8) | (row >= 32), row % 32, -1)
    sels = np.concatenate([row == q // P, row == (q[:, :4 * P] // P) * 2 + (q[:, :4 * P] % P) // 64],
                          axis=1).astype(np.float32)
    cons = np.concatenate([np.ones((P, P)), i > j, i <= j, i == j, inv], axis=1).astype(np.float32)
    assert cons.shape == (P, NC)

    xin = np.ascontiguousarray(a["x"][0].reshape(T, KT, P).transpose(2, 1, 0))
    arrays = dict(w8=w8, w22=w22, wcond=wcond, wdt=wdt, wpool=wpool, vecs=vecs, cons=cons, atts=atts, sels=sels, xin=xin)
    arrays = {n: np.ascontiguousarray(v) for n, v in arrays.items()}
    nc = bacc.Bacc("TRN2", target_bir_lowering=False, num_devices=1, dynamic_dma_scratch_size=1024)
    args = [nc.dram_tensor(n, v.shape, F32, kind="ExternalInput").ap() for n, v in arrays.items()]
    out = nc.dram_tensor("out", (P, KT, T), F32, kind="ExternalOutput").ap()
    hybrid_blocks(nc, *args, out)
    r = run_bass_kernel_spmd(nc, [arrays], core_ids=[0])
    return np.ascontiguousarray(r.results[0]["out"].transpose(2, 1, 0).reshape(1, T, D))
```
